# Optimizing a Trainium2 kernel written in Bass

```python
import math
import jax, jax.numpy as jnp
from jax import lax
import numpy as np

D_MODEL = 1024
BATCH = 1
SEQ = 1024
DEPTH = 1

MIX_WIDTH = D_MODEL
DA_HEADS = 4
DA_QK_DIM = 64
DA_V_DIM = 2 * DA_QK_DIM
DA_WIDTH = DA_HEADS * DA_V_DIM
Q_BLOCK = 128
ML_HEADS = 4
ML_QK_DIM = 64
ML_V_DIM = 128
ML_WIDTH = ML_HEADS * ML_V_DIM
ML_CONV = 4
ML_CHUNK = 64
FORGET_BIAS_LO = 3.0
FORGET_BIAS_HI = 6.0
REL_BUCKETS = 32
REL_MAX_DIST = 128
N_EXPERTS = 32
TOP_K = 4
D_FF = D_MODEL
SWIGLU_LIMIT = 7.0
SWIGLU_ALPHA = 1.702
MOE_BLOCK = 128
NORM_EPS = 1e-5
DA_Q_COLS = DA_HEADS * 2 * DA_QK_DIM
DA_K_COLS = DA_HEADS * 2 * DA_QK_DIM
DA_V_COLS = DA_WIDTH
ML_Q_COLS = ML_HEADS * ML_QK_DIM
ML_K_COLS = ML_HEADS * ML_QK_DIM
ML_V_COLS = ML_WIDTH
ML_O_COLS = ML_WIDTH
ML_GATE_COLS = 2 * ML_HEADS
IN_COLS = DA_Q_COLS + DA_K_COLS + DA_V_COLS + ML_Q_COLS + ML_K_COLS + ML_V_COLS + ML_O_COLS + ML_GATE_COLS

kernel_name = "hymba_diffattn_mlstm_moe_block"

def rms_norm(x, g):
    xf = x.astype(jnp.float32)
    y = xf * lax.rsqrt(jnp.mean(xf * xf, axis=-1, keepdims=True) + NORM_EPS)
    return (y * g.astype(jnp.float32)).astype(x.dtype)

def head_rms_norm(x, g):
    H, d = x.shape[-2], x.shape[-1]
    return rms_norm(x, g.reshape(H, d))

def lambda_init_fn(layer):
    return 0.8 - 0.6 * math.exp(-0.3 * layer)

def t5_bucket(rel):
    n = jnp.maximum(rel, 0)
    max_exact = REL_BUCKETS // 2
    nf = jnp.maximum(n, 1).astype(jnp.float32)
    large = max_exact + (jnp.log(nf / max_exact) / math.log(REL_MAX_DIST / max_exact)
                         * (REL_BUCKETS - max_exact)).astype(jnp.int32)
    large = jnp.minimum(large, REL_BUCKETS - 1)
    return jnp.where(n < max_exact, n, large)

def diff_attention(q, k, v, table, lam):
    S = q.shape[1]
    q = jnp.transpose(q, (0, 2, 3, 1, 4))
    k = jnp.transpose(k, (0, 2, 3, 1, 4))
    v = jnp.transpose(v, (0, 2, 1, 3))
    scale = DA_QK_DIM ** -0.5
    table = table.astype(jnp.float32)
    outs = []
    for blk in range(S // Q_BLOCK):
        qs = blk * Q_BLOCK
        end = qs + Q_BLOCK
        logits = jnp.einsum('bhmqd,bhmkd->bhmqk', q[:, :, :, qs:end], k[:, :, :, :end]).astype(jnp.float32) * scale
        rel = (qs + jnp.arange(Q_BLOCK))[:, None] - jnp.arange(end)[None, :]
        bias = jnp.transpose(table[t5_bucket(rel)], (2, 0, 1))
        logits = jnp.where(rel >= 0, logits + bias[None, :, None], -jnp.inf)
        p = jax.nn.softmax(logits, axis=-1)
        a = p[:, :, 0] - lam * p[:, :, 1]
        outs.append(jnp.einsum('bhqk,bhkd->bhqd', a.astype(v.dtype), v[:, :, :end]))
    out = jnp.concatenate(outs, axis=2)
    return jnp.transpose(out, (0, 2, 1, 3))

def causal_conv(x, w, b):
    K = w.shape[0]
    S = x.shape[1]
    xp = jnp.pad(x, ((0, 0), (K - 1, 0), (0, 0)))
    y = b
    for tap in range(K):
        y = y + xp[:, tap:tap + S] * w[tap]
    return y

def mlstm_chunkwise(q, k, v, log_i, log_f):
    B, H, S, dk = q.shape
    dv = v.shape[-1]
    L = ML_CHUNK
    nc = S // L

    def chunks(a):
        return jnp.moveaxis(a.reshape(a.shape[:2] + (nc, L) + a.shape[3:]), 2, 0)

    causal = jnp.tril(jnp.ones((L, L), dtype=bool))

    def step(carry, inp):
        C, n, m = carry
        qc, kc, vc, li, lf = inp
        b = jnp.cumsum(lf, axis=-1)
        dlog = jnp.where(causal, b[..., :, None] - b[..., None, :] + li[..., None, :], -jnp.inf)
        inter = b + m[..., None]
        m_t = jnp.maximum(jnp.max(dlog, axis=-1), inter)
        w_intra = jnp.exp(dlog - m_t[..., None])
        w_inter = jnp.exp(inter - m_t)
        s = jnp.einsum('bhtd,bhjd->bhtj', qc, kc) * w_intra
        num = jnp.einsum('bhtj,bhje->bhte', s, vc) + w_inter[..., None] * jnp.einsum('bhtd,bhde->bhte', qc, C)
        den = jnp.sum(s, axis=-1) + w_inter * jnp.einsum('bhtd,bhd->bht', qc, n)
        h = num / jnp.maximum(jnp.abs(den), jnp.exp(-m_t))[..., None]
        g = b[..., -1]
        wlog = g[..., None] - b + li
        m_new = jnp.maximum(g + m, jnp.max(wlog, axis=-1))
        decay = jnp.exp(g + m - m_new)
        wk = jnp.exp(wlog - m_new[..., None])
        C_new = decay[..., None, None] * C + jnp.einsum('bhj,bhjd,bhje->bhde', wk, kc, vc)
        n_new = decay[..., None] * n + jnp.einsum('bhj,bhjd->bhd', wk, kc)
        return (C_new, n_new, m_new), h

    init = (jnp.zeros((B, H, dk, dv), jnp.float32), jnp.zeros((B, H, dk), jnp.float32),
            jnp.zeros((B, H), jnp.float32))
    _, hs = lax.scan(step, init, (chunks(q), chunks(k), chunks(v), chunks(log_i), chunks(log_f)))
    return jnp.moveaxis(hs, 0, 2).reshape(B, H, S, dv)

def moe(h, router_w, router_b, w_gu, b_gu, w_down, b_down):
    B, S, D = h.shape
    T = B * S
    xt = h.reshape(T, D)
    logits = (xt @ router_w + router_b).astype(jnp.float32)
    top_val, top_idx = lax.top_k(logits, TOP_K)
    gates = jax.nn.softmax(top_val, axis=-1)
    P = T * TOP_K
    e_flat = top_idx.reshape(P)
    tok_flat = jnp.repeat(jnp.arange(T, dtype=jnp.int32), TOP_K)
    g_flat = gates.reshape(P)
    order = jnp.argsort(e_flat)
    e_sorted = e_flat[order]
    counts = jnp.bincount(e_flat, length=N_EXPERTS)
    padded = (counts + MOE_BLOCK - 1) // MOE_BLOCK * MOE_BLOCK
    start = jnp.cumsum(counts) - counts
    pstart = jnp.cumsum(padded) - padded
    dest = pstart[e_sorted] + (jnp.arange(P) - start[e_sorted])
    n_rows = (P + MOE_BLOCK - 1) // MOE_BLOCK * MOE_BLOCK + N_EXPERTS * MOE_BLOCK
    n_blocks = n_rows // MOE_BLOCK
    row_tok = jnp.zeros((n_rows,), jnp.int32).at[dest].set(tok_flat[order])
    row_gate = jnp.zeros((n_rows,), jnp.float32).at[dest].set(g_flat[order])
    block_expert = jnp.minimum(
        jnp.searchsorted(jnp.cumsum(padded), jnp.arange(n_blocks) * MOE_BLOCK, side='right'),
        N_EXPERTS - 1)

    def expert_block(args):
        rows, e = args
        xb = xt[rows]
        gu = xb @ w_gu[e] + b_gu[e]
        glu = jnp.minimum(gu[:, :D_FF], SWIGLU_LIMIT)
        lin = jnp.clip(gu[:, D_FF:], -SWIGLU_LIMIT, SWIGLU_LIMIT)
        act = glu * jax.nn.sigmoid(SWIGLU_ALPHA * glu) * (lin + 1)
        return act @ w_down[e] + b_down[e]

    ys = lax.map(expert_block, (row_tok.reshape(n_blocks, MOE_BLOCK), block_expert)).reshape(n_rows, D)
    y = jax.ops.segment_sum(ys * row_gate[:, None].astype(ys.dtype), row_tok, num_segments=T)
    return y.reshape(B, S, D)

def setup_inputs(seed: int = 0) -> dict:
    key = jax.random.key(seed)
    ks = jax.random.split(key, 24)

    def nrm(k, shape, s):
        return s * jax.random.normal(k, shape, jnp.float32)

    forget_b = jnp.linspace(FORGET_BIAS_LO, FORGET_BIAS_HI, ML_HEADS, dtype=jnp.float32)[None] + nrm(ks[10], (DEPTH, ML_HEADS), 0.1)
    input_b = nrm(ks[11], (DEPTH, ML_HEADS), 0.1)
    return {
        "x": jax.random.normal(ks[0], (BATCH, SEQ, D_MODEL), jnp.float32),
        "norm_attn_g": 1.0 + nrm(ks[1], (DEPTH, D_MODEL), 0.02),
        "w_in": nrm(ks[2], (DEPTH, D_MODEL, IN_COLS), D_MODEL ** -0.5),
        "rel_bias_table": nrm(ks[3], (REL_BUCKETS, DA_HEADS), 0.5),
        "lambda_q1": nrm(ks[4], (DEPTH, DA_QK_DIM), 0.1),
        "lambda_k1": nrm(ks[5], (DEPTH, DA_QK_DIM), 0.1),
        "lambda_q2": nrm(ks[6], (DEPTH, DA_QK_DIM), 0.1),
        "lambda_k2": nrm(ks[7], (DEPTH, DA_QK_DIM), 0.1),
        "diff_norm_g": 1.0 + nrm(ks[8], (DEPTH, DA_WIDTH), 0.02),
        "mlstm_conv_w": nrm(ks[9], (DEPTH, ML_CONV, ML_Q_COLS + ML_K_COLS), 0.5),
        "mlstm_conv_b": nrm(ks[12], (DEPTH, ML_Q_COLS + ML_K_COLS), 0.02),
        "mlstm_gate_b": jnp.concatenate([input_b, forget_b], axis=-1),
        "mlstm_o_b": nrm(ks[13], (DEPTH, ML_WIDTH), 0.1),
        "mlstm_norm_g": 1.0 + nrm(ks[14], (DEPTH, ML_WIDTH), 0.02),
        "w_out": nrm(ks[15], (DEPTH, MIX_WIDTH, D_MODEL), MIX_WIDTH ** -0.5),
        "norm_ffn_g": 1.0 + nrm(ks[16], (DEPTH, D_MODEL), 0.02),
        "router_w": nrm(ks[17], (DEPTH, D_MODEL, N_EXPERTS), D_MODEL ** -0.5),
        "router_b": nrm(ks[18], (DEPTH, N_EXPERTS), 0.01),
        "expert_w_gu": nrm(ks[19], (DEPTH, N_EXPERTS, D_MODEL, 2 * D_FF), D_MODEL ** -0.5),
        "expert_b_gu": nrm(ks[20], (DEPTH, N_EXPERTS, 2 * D_FF), 0.01),
        "expert_w_down": nrm(ks[21], (DEPTH, N_EXPERTS, D_FF, D_MODEL), D_FF ** -0.5),
        "expert_b_down": nrm(ks[22], (DEPTH, N_EXPERTS, D_MODEL), 0.01),
        "final_norm_g": 1.0 + nrm(ks[23], (D_MODEL,), 0.02),
    }

def reference(x, norm_attn_g, w_in, rel_bias_table, lambda_q1, lambda_k1, lambda_q2, lambda_k2,
              diff_norm_g, mlstm_conv_w, mlstm_conv_b, mlstm_gate_b, mlstm_o_b, mlstm_norm_g,
              w_out, norm_ffn_g, router_w, router_b, expert_w_gu, expert_b_gu, expert_w_down,
              expert_b_down, final_norm_g):
    B, S, _ = x.shape
    split_at = list(np.cumsum([DA_Q_COLS, DA_K_COLS, DA_V_COLS, ML_Q_COLS + ML_K_COLS, ML_V_COLS, ML_O_COLS]))
    for l in range(DEPTH):
        h = rms_norm(x, norm_attn_g[l])
        proj = h @ w_in[l]
        da_q, da_k, da_v, ml_qk, ml_v, ml_o, ml_g = jnp.split(proj, split_at, axis=-1)

        lam_init = lambda_init_fn(l)
        lam = (jnp.exp(jnp.sum(lambda_q1[l] * lambda_k1[l])) - jnp.exp(jnp.sum(lambda_q2[l] * lambda_k2[l]))
               + lam_init).astype(jnp.float32)
        a_out = diff_attention(da_q.reshape(B, S, DA_HEADS, 2, DA_QK_DIM),
                               da_k.reshape(B, S, DA_HEADS, 2, DA_QK_DIM),
                               da_v.reshape(B, S, DA_HEADS, DA_V_DIM), rel_bias_table, lam)
        a_out = head_rms_norm(a_out, diff_norm_g[l]) * (1.0 - lam_init)

        qk = jax.nn.silu(causal_conv(ml_qk, mlstm_conv_w[l], mlstm_conv_b[l]))
        ml_q = qk[..., :ML_Q_COLS].reshape(B, S, ML_HEADS, ML_QK_DIM).transpose(0, 2, 1, 3).astype(jnp.float32)
        ml_k = qk[..., ML_Q_COLS:].reshape(B, S, ML_HEADS, ML_QK_DIM).transpose(0, 2, 1, 3).astype(jnp.float32)
        ml_k = ml_k * (ML_QK_DIM ** -0.5)
        ml_vh = ml_v.reshape(B, S, ML_HEADS, ML_V_DIM).transpose(0, 2, 1, 3).astype(jnp.float32)
        gate_pre = (ml_g + mlstm_gate_b[l]).astype(jnp.float32)
        log_i = jnp.transpose(gate_pre[..., :ML_HEADS], (0, 2, 1))
        log_f = jnp.transpose(jax.nn.log_sigmoid(gate_pre[..., ML_HEADS:]), (0, 2, 1))
        m_out = mlstm_chunkwise(ml_q, ml_k, ml_vh, log_i, log_f)
        m_out = jnp.transpose(m_out, (0, 2, 1, 3)).astype(x.dtype)
        o_gate = jax.nn.sigmoid(ml_o + mlstm_o_b[l]).reshape(B, S, ML_HEADS, ML_V_DIM)
        m_out = head_rms_norm(m_out, mlstm_norm_g[l]) * o_gate

        mixed = jnp.concatenate([a_out.reshape(B, S, DA_WIDTH), m_out.reshape(B, S, ML_WIDTH)], axis=-1)
        x = x + mixed @ w_out[l]

        x = x + moe(rms_norm(x, norm_ffn_g[l]), router_w[l], router_b[l], expert_w_gu[l],
                    expert_b_gu[l], expert_w_down[l], expert_b_down[l])
    return rms_norm(x, final_norm_g)


_drawn_inputs = setup_inputs


def setup_inputs(seed=0):
    import zlib

    import numpy as np

    out = dict(_drawn_inputs(seed))
    spreads = {}
    factors = {'expert_b_gu': 8.0, 'expert_b_down': 8.0, 'final_norm_g': 2.91}
    for name, (base, spread) in spreads.items():
        noise = np.random.default_rng([zlib.crc32(name.encode()), seed]).standard_normal(out[name].shape)
        drawn = base * np.exp(spread * noise) if base else spread * noise
        out[name] = __import__('jax').numpy.asarray(drawn.astype(out[name].dtype))
    for name, factor in factors.items():
        out[name] = (out[name] * factor).astype(out[name].dtype)
    return out
```

```python
import math
from contextlib import ExitStack

import numpy as np
import concourse.bass as bass
from concourse import mybir

F32 = mybir.dt.float32
I32 = mybir.dt.int32
U32 = mybir.dt.uint32
ALU = mybir.AluOpType
ACT = mybir.ActivationFunctionType
AX = mybir.AxisListType.X

P = 128
SEQ = 1024
D = 1024
NT = SEQ // P
KD = D // P
HALF = 512
DAH, DQ, DV = 4, 64, 128
MLH = 4
IN_COLS = 3080
EPS = 1e-5
REL_BUCKETS, REL_MAX_DIST = 32, 128
STRIP = SEQ + P - 1
MASKED = -1e30
N_EXP, TOP_K, D_FF = 32, 4, 1024
NF = D_FF // P
LIMIT, ALPHA = 7.0, 1.702
ITEM = 256
LISTS = SEQ // P
MAX_EXTRA = 15
ITEMS = N_EXP + MAX_EXTRA
ROUNDS = SEQ // ITEM - 1
WIDTHS = list(range(64, ITEM + 1, 16))
NO_ROW = 1 << 20
V_GA, V_GF, V_GD, V_GM, V_CW, V_CB, V_OB, V_ROWS = 0, 8, 16, 20, 24, 40, 44, 48
LAM_INIT = 0.8 - 0.6 * math.exp(-0.3 * 0)


def bucket_rows():
    rel = np.arange(SEQ - 1, -1, -1)
    exact = REL_BUCKETS // 2
    large = exact + (np.log(np.maximum(rel, 1).astype(np.float32) / exact) / math.log(REL_MAX_DIST / exact)
                     * (REL_BUCKETS - exact)).astype(np.int32)
    bucket = np.where(rel < exact, rel, np.minimum(large, REL_BUCKETS - 1))
    return (np.arange(REL_BUCKETS)[:, None] == bucket[None, :]).astype(np.float32)


class Steps:

    def __init__(self, eng, sem):
        self.eng, self.sem, self.n, self.base = eng, sem, 0, 0

    def do(self, ins):
        self.n += 1
        ins.then_inc(self.sem, 1)
        self.eng.wait_ge(self.sem, self.base + self.n)


def build(nc, x, norm_attn_g, w_in, rel_bias_table, lambda_q1, lambda_k1, lambda_q2, lambda_k2,
          diff_norm_g, mlstm_conv_w, mlstm_conv_b, mlstm_gate_b, mlstm_o_b, mlstm_norm_g, w_out,
          norm_ffn_g, router_w, router_b, expert_w_gu, expert_b_gu, expert_w_down, expert_b_down,
          final_norm_g, buckets, out):
    x_rows = x.rearrange("b (t p) d -> (b t) p d", p=P)
    out_rows = out.rearrange("b (t p) d -> (b t) p d", p=P)
    w_in_k = w_in.rearrange("l (k p) n -> p (l k) n", p=P)
    w_out_k = w_out.rearrange("l (k p) n -> p (l k) n", p=P)
    w_gu = expert_w_gu.rearrange("l e (k p) (h f) -> (l e) h p k f", p=P, h=2)
    w_down = expert_w_down.rearrange("l e (k p) n -> (l e) p k n", p=P)
    strip_dram = nc.dram_tensor("strip_dram", [DAH, STRIP + 1], F32).ap()
    h2_dram = nc.dram_tensor("h2_dram", [SEQ, D], F32).ap()
    y_dram = nc.dram_tensor("y_dram", [SEQ * TOP_K, D], F32).ap()
    list_dram = nc.dram_tensor("list_dram", [P * N_EXP * LISTS, 1], I32).ap()

    with ExitStack() as ctx:
        def sb(name, shape, dt=F32):
            return ctx.enter_context(nc.sbuf_tensor(name, shape, dt))

        def sem(name):
            return ctx.enter_context(nc.semaphore(name))

        PS = ctx.enter_context(nc.psum_tensor("PS", [P, 8, HALF], F32))

        def bank(b):
            return PS[:, b, :]

        def banks2(b):
            return PS[:, b:b + 2, :].rearrange("p b n -> p (b n)")

        unit = [sb(f"unit{i}", [P, 4128 if i == 0 else 4096]) for i in range(6)]
        pairA, pairB = sb("pairA", [P, 8192]), sb("pairB", [P, 8192])
        unit10, unit11 = sb("unit10", [P, 4096]), sb("unit11", [P, 4096])
        scratch = sb("scratch", [P, 1024])

        def kn(t, k=KD):
            return t.rearrange("p (k n) -> p k n", k=k)

        group_w = [kn(unit[i][:, 0:4096]) for i in (2, 3, 0, 1, 4, 5)]
        x_raw = kn(pairB[:, :])
        hT = kn(pairA[:, :])
        one_hot = unit11[0:REL_BUCKETS, 0:SEQ]
        strip_row = unit11[0:DAH, SEQ:SEQ + STRIP + 1]
        gate_w = kn(unit11[:, 3600:3888])
        vec_rows = unit11[0:V_ROWS, 3888:4016]
        ml_raw = kn(unit10[:, :], 4)
        ml_qk = kn(unit[2][:, :], 4)
        ml_sig = kn(unit[3][:, :], 4)
        da_q = kn(unit11[:, :], DAH)
        da_k = kn(pairB[:, 0:4096], DAH)
        da_v = kn(pairB[:, 4096:8192])
        gate_rows = pairB[:, 4096:5120]
        row_a, row_b, row_c = (pairB[0:MLH, 5120 + 1024 * i:6144 + 1024 * i] for i in range(3))
        row_g = pairB[0:MLH, 4096:5120]
        ml_v = unit[0][:, 0:NT * MLH * (DV + 1)].rearrange("p (t h d) -> p t h d", t=NT, h=MLH)
        o_gate = kn(unit[1][:, :], 4)
        m_wide = kn(unit[3][:, :], MLH)
        ml_decay = kn(unit10[:, 0:1024], 2)
        ml_w = kn(unit10[:, 1024:2048], 2)
        ml_e = kn(unit10[:, 2048:2304], 2)
        ml_h = unit10[:, 2304:2820].rearrange("p (h d) -> p h d", h=MLH)
        ml_hr = kn(unit10[:, 2820:3332], MLH)
        ml_sq = kn(unit10[:, 3332:3844], MLH)
        above = unit10[:, 3844:3972]
        pick = kn(scratch[:, 0:512], 4)
        lam_in = kn(scratch[:, 512:768], 4)
        flip = scratch[:, 768:768 + P]
        strip = kn(unit[4][:, :], DAH)
        prob = [[u[:, 0:1024], u[:, 1024:2048]] for u in (unit[3], unit10)]
        probT = kn(unit[3][:, 2048:3072], 2)
        da_o = kn(unit10[:, 2048:2560], DAH)
        da_sq = kn(unit10[:, 2560:3072], DAH)
        mixT = kn(pairA[:, :])
        w_o = [kn(unit[5][:, :], 4), kn(unit[2][:, :], 4)]
        x1 = kn(pairB[:, :])
        h2 = kn(unit10[:, 0:2048], 2)
        h2T = [kn(unit10[:, 2048 + 1024 * i:3072 + 1024 * i]) for i in range(2)]
        x_again = kn(unit11[:, 0:2048], 2)
        b_gu_rows = unit11[0:N_EXP, 2048:4096]
        chosen = scratch[:, :].rearrange("p (t c e) -> p t c e", t=NT, c=TOP_K)
        b_down = pairA[0:N_EXP, 6144:7168]
        g_allT = kn(pairA[0:N_EXP, 7168:8192])
        n_flags = ROUNDS * N_EXP
        flag, pos, pos2, val_e, val_c, val_n = (unit10[0:1, n_flags * i:n_flags * (i + 1)] for i in range(6))
        eq = kn(unit10[0:1, 1024:1024 + MAX_EXTRA * n_flags], MAX_EXTRA)
        pick_v = kn(unit10[0:1, 2560:2560 + MAX_EXTRA * n_flags], MAX_EXTRA)
        order = kn(unit11[0:1, 2048:2048 + MAX_EXTRA * n_flags], MAX_EXTRA)
        got = unit11[0:1, 3584:3584 + 64]
        xg = kn(pairA[:, 0:2048], 2)
        xT = kn(pairA[:, 2048:4096])
        actT = kn(pairA[:, 4096:6144])
        y_rows = kn(pairA[:, 6144:8192], 2)
        gu_w = [unit[i][:, 0:4096].rearrange("p (h k f) -> p h k f", h=2, k=KD) for i in range(4)]
        down_w = [kn(unit[4 + c // 2][:, 2048 * (c % 2):2048 * (c % 2) + 2048]) for c in range(4)]
        yT = kn(unit10[:, 2048:4096])
        glu_t = kn(unit10[:, 0:512], 2)
        glu_s = kn(unit10[:, 512:1024], 2)
        lin_b = kn(unit10[:, 1024:1536], 2)
        lin_c = kn(unit10[:, 1536:2048], 2)
        y_in = [unit[i][:, 0:4096].rearrange("p (c d) -> p c d", c=TOP_K) for i in range(4)]
        gain_wide = unit11[:, 0:1024]
        out_sb = kn(unit11[:, 1024:4096], 3)

        ident, ones, before = sb("ident", [P, P]), sb("ones", [P, P]), sb("before", [P, P])
        vec = sb("vec", [P, V_ROWS])
        gd_scaled = sb("gd_scaled", [P, DAH])
        gate_bias = sb("gate_bias", [64, 1])
        neg_half = sb("neg_half", [P, NT])
        ssq, rstd = sb("ssq", [P, NT]), sb("rstd", [P, NT])
        table = sb("table", [REL_BUCKETS, DAH])
        lam = sb("lam", [P, 4])
        a_col, em_col = sb("a_col", [P, NT, MLH]), sb("em_col", [P, NT, MLH])
        small = sb("small", [P, 32])
        rw = sb("rw", [P, KD, N_EXP])
        rb_wide = sb("rb_wide", [P, N_EXP])
        lanes = sb("lanes", [P, N_EXP])
        lg, top8 = sb("lg", [P, N_EXP]), sb("top8", [P, 8])
        idx8 = sb("idx8", [P, 8], U32)
        idxf = sb("idxf", [P, NT, TOP_K])
        gate = sb("gate", [P, NT, TOP_K])
        mask = sb("mask", [P, NT, N_EXP])
        g_all = sb("g_all", [P, NT, N_EXP])
        slot = sb("slot", [P, NT, TOP_K])
        slot_i, slot_lo = sb("slot_i", [P, NT, TOP_K], I32), sb("slot_lo", [P, NT, TOP_K], I32)
        where = sb("where", [P, NT, TOP_K], I32)
        row_id = sb("row_id", [P, NT, TOP_K], I32)
        y_idx, x_idx = sb("y_idx", [P, N_EXP * LISTS], I32), sb("x_idx", [P, N_EXP * LISTS], I32)
        cur_x, cur_y = sb("cur_x", [P, 2], I32), sb("cur_y", [P, 2], I32)
        b_gu = sb("b_gu", [P, N_EXP, 2 * NF])
        cur_b = sb("cur_b", [P, 2 * NF])
        counts = sb("counts", [P, N_EXP])
        item_e, item_col, item_n = (sb(n, [1, ITEMS + 1], I32) for n in ("item_e", "item_col", "item_n"))
        n_items = sb("n_items", [1, 1], I32)

        x_in = [sem(f"x_in{t}") for t in range(NT)]
        group_in = [sem(f"group_in{g}") for g in range(6)]
        (small_in, consts, vec_ps, vec_ready, strip_ps, strip_row_ready, strip_out, strip_in, mean_sq,
         rstd_ready, x_scaled, x_turned, hT_ready, proj_done, proj_evac, conv_done, sig_done, qk_done,
         log_f_in, log_f_part, em_in, em_ready, rows_ready, cols_ps, cols_ready, wide_ps, wide_ready,
         dve_step, act_step, pool_step) = (sem(n) for n in (
             "small_in", "consts", "vec_ps", "vec_ready", "strip_ps", "strip_row_ready", "strip_out",
             "strip_in", "mean_sq", "rstd_ready", "x_scaled", "x_turned", "hT_ready", "proj_done",
             "proj_evac", "conv_done", "sig_done", "qk_done", "log_f_in", "log_f_part", "em_in", "em_ready",
             "rows_ready", "cols_ps", "cols_ready", "wide_ps", "wide_ready", "dve_step", "act_step",
             "pool_step"))
        (ml_s_done, ml_e_ready, ml_d_ready, ml_w_ready, ml_h_done, ml_h_read, ml_norm_ready, ml_turned,
         ml_mixed, da_logits, da_max, da_exp, da_a_ready, da_aT_ps, da_aT_ready, da_o_done, da_o_read,
         da_norm_ready, da_turned, da_mixed, w_out_in0, w_out_in1) = (sem(n) for n in (
             "ml_s_done", "ml_e_ready", "ml_d_ready", "ml_w_ready", "ml_h_done", "ml_h_read",
             "ml_norm_ready", "ml_turned", "ml_mixed", "da_logits", "da_max", "da_exp", "da_a_ready",
             "da_aT_ps", "da_aT_ready", "da_o_done", "da_o_read", "da_norm_ready", "da_turned", "da_mixed",
             "w_out_in0", "w_out_in1"))
        x_again_in = [sem(f"x_again_in{i}") for i in range(2)]
        h2_out = [sem(f"h2_out{i}") for i in range(2)]
        (out_proj_done, x1_ready, h2_ready, h2_turned, h2T_ready, logits_done, top_ready, gate_exp,
         chosen_ready, pos_ps, slots_ready, where_ready, list_clear, list_out, list_in, g_turned,
         g_allT_ready, down_bias_done, x1_full, b_gu_turned, b_gu_ready, b_down_in, items_ready,
         moe_clear, row_ids) = (sem(n) for n in (
             "out_proj_done", "x1_ready", "h2_ready", "h2_turned", "h2T_ready", "logits_done", "top_ready",
             "gate_exp", "chosen_ready", "pos_ps", "slots_ready", "where_ready", "list_clear", "list_out",
             "list_in", "g_turned", "g_allT_ready", "down_bias_done", "x1_full", "b_gu_turned",
             "b_gu_ready", "b_down_in", "items_ready", "moe_clear", "row_ids"))
        gu_in = [sem(f"gu_in{c}") for c in range(4)]
        down_in = [sem(f"down_in{c}") for c in range(4)]
        (cur_x_ready, cur_y_ready, cur_b_ready, xg_in, xT_ps, xT_evac, gu_done, glu_read, lin_read,
         sig_ready, act_ready, yT_ps, yT_evac, y_ps, y_evac, y_out, gain_in, y_sum, out_ready) = (
            sem(n) for n in (
                "cur_x_ready", "cur_y_ready", "cur_b_ready", "xg_in", "xT_ps", "xT_evac", "gu_done",
                "glu_read", "lin_read", "sig_ready", "act_ready", "yT_ps", "yT_evac", "y_ps", "y_evac", "y_out",
                "gain_in", "y_sum", "out_ready"))
        lam_ready, lam_exp, item_iotas, tail_step, b_gu_in, v_ones = (sem(n) for n in (
            "lam_ready", "lam_exp", "item_iotas", "tail_step", "b_gu_in", "v_ones"))
        gate_bias_clear, pool_waited, y_sent, strip_flipped, strip_ready = (sem(n) for n in (
            "gate_bias_clear", "pool_waited", "y_sent", "strip_flipped", "strip_ready"))
        y_back = [sem(f"y_back{i}") for i in range(4)]
        out_sent = [sem(f"out_sent{i}") for i in range(3)]

        def wide(ap, n):
            return ap.unsqueeze(len(ap.shape)).broadcast_to(list(ap.shape) + [n])

        def again(ap, n):
            return ap.unsqueeze(1).broadcast_to([ap.shape[0], n, ap.shape[1]])

        QKM, Q, K, V, MV, MO, GATE = range(7)
        outs = [(QKM, h, m) for h in range(2) for m in range(4)] + [(GATE, 0, 0), (GATE, 1, 0)]
        for g in (Q, K):
            outs += [(g, h, m) for h in range(2) for m in range(4)]
        outs += [(V, 0, t) for t in range(NT)] + [(MV, 0, t) for t in range(NT)]
        outs += [(MO, h, m) for h in range(2) for m in range(4)]
        N_OUTS = len(outs)
        after_group = {g: 1 + max(o for o, (k, _, _) in enumerate(outs) if k == g) for g in range(7)}

        ml_units = [(t, h, list(range(j, min(j + 4, t + 1)))) for t in range(NT) for h in range(MLH)
                    for j in range(0, t + 1, 4)]
        ml_tile_end = [max(u for u, (t, _, _) in enumerate(ml_units) if t == n) + 1 for n in range(NT)]
        da_units = [(t, h) for t in range(NT) for h in range(DAH)]
        da_groups = []
        for t, h in da_units:
            da_groups.append([list(range(j, min(j + 4, t + 1))) for j in range(0, t + 1, 4)])
        N_SMALL = 7 + 2 + 1 + 1 + 4 + 1 + 1 + 2

        block = ctx.enter_context(nc.Block())

        @block.sync
        def _(sp):
            for t in range(NT):
                sp.dma_start(x_raw[:, t, :], x_rows[t]).then_inc(x_in[t], 16)
            first_col = [1536, 0, 512, 1024, 2048, 2560]
            for g in range(6):
                c = first_col[g]
                sp.dma_start(group_w[g], w_in_k[:, :, c:c + HALF]).then_inc(group_in[g], 16)
            sp.wait_ge(strip_row_ready, 3)
            sp.dma_start(strip_dram, strip_row).then_inc(strip_out, 16)
            sp.wait_ge(strip_out, 16)
            sp.wait_ge(proj_done, after_group[MV])
            shifted = bass.AP(strip_dram.tensor, 0, [[1, P], [STRIP + 1, DAH], [1, SEQ]])
            sp.dma_start(strip, shifted).then_inc(strip_in, 16)
            sp.wait_ge(proj_done, after_group[MO])
            sp.dma_start(w_o[0], w_out_k[:, 0:4, :]).then_inc(w_out_in0, 16)
            sp.wait_ge(ml_h_done, len(ml_units))
            sp.dma_start(w_o[1], w_out_k[:, 4:8, :]).then_inc(w_out_in1, 16)

            def load_gu(c, e):
                for h in range(2):
                    sp.dma_start(gu_w[c][:, h], w_gu[e, h, :, :, 256 * c:256 * c + 256]).then_inc(gu_in[c], 16)

            def load_down(c, e):
                sp.dma_start(down_w[c], w_down[e, :, :, 256 * c:256 * c + 256]).then_inc(down_in[c], 16)

            load_gu(0, 0)
            sp.wait_ge(ml_mixed, NT)
            load_gu(1, 0)
            sp.wait_ge(da_mixed, NT)
            load_gu(3, 0)
            load_down(0, 0)
            load_down(1, 0)
            for t in range(2):
                sp.dma_start(x_again[:, t, :], x_rows[t]).then_inc(x_again_in[t], 16)
            sp.dma_start(b_gu_rows, expert_b_gu.rearrange("l e f -> (l e) f")).then_inc(b_gu_in, 16)
            for t in range(NT):
                sp.wait_ge(h2_ready, t + 1)
                sp.dma_start(h2_dram[P * t:P * t + P, :], h2[:, t % 2, :]).then_inc(h2_out[t % 2], 16)
                if t + 2 < NT:
                    sp.dma_start(x_again[:, t % 2, :], x_rows[t + 2]).then_inc(x_again_in[t % 2], 16)
            sp.wait_ge(out_proj_done, NT)
            load_gu(2, 0)
            load_down(2, 0)
            load_down(3, 0)
            sp.dma_start(b_down, expert_b_down.rearrange("l e d -> (l e) d")).then_inc(b_down_in, 16)
            sp.wait_ge(list_out, 16 * NT * TOP_K)
            sp.dma_start(y_idx[:, :], list_dram.rearrange("(p c) o -> p (c o)", p=P)).then_inc(list_in, 16)

            def item_weights(i, e):
                for c in range(4):
                    sp.wait_ge(gu_done, 8 * (i - 1) + 2 * c + 2)
                    load_gu(c, e)
                for c in range(4):
                    sp.wait_ge(yT_ps, 8 * (i - 1) + 2 * c + 3)
                    load_down(c, e)

            with sp.Fori(1, N_EXP) as i:
                item_weights(i, i)
            sp.wait_ge(items_ready, 1)
            last = sp.value_load(n_items[0:1, 0:1], min_val=N_EXP, max_val=ITEMS)
            with sp.Fori(N_EXP, ITEMS) as i:
                with sp.If(i < last):
                    item_weights(i, sp.value_load(item_e[0:1, bass.ds(i, 1)], min_val=0, max_val=N_EXP - 1))
            sp.wait_ge(y_sent, last + 1)
            sp.dma_start(gain_wide, final_norm_g.partition_broadcast(P)).then_inc(gain_in, 16)
            for t in range(NT):
                if t >= 4:
                    sp.wait_ge(y_sum, t - 3)
                sp.dma_start(y_in[t % 4], y_dram[P * TOP_K * t:P * TOP_K * (t + 1), :]
                             .rearrange("(p c) d -> p c d", c=TOP_K)).then_inc(y_back[t % 4], 16)
                if t >= 3:
                    sp.wait_ge(out_ready, t - 2)
                    sp.dma_start(out_rows[t - 3], out_sb[:, (t - 3) % 3, :]).then_inc(out_sent[(t - 3) % 3], 16)
            for t in range(NT - 3, NT):
                sp.wait_ge(out_ready, t + 1)
                sp.dma_start(out_rows[t], out_sb[:, t % 3, :]).then_inc(out_sent[t % 3], 16)
            for i in range(3):
                sp.wait_ge(out_sent[i], 16 * len(range(i, NT, 3)))

        @block.gpsimd
        def _(pool):
            step = Steps(pool, pool_step)
            pool.memset(gate_w, 0.0).then_inc(consts, 1)
            pool.memset(gate_bias[:, :], 0.0).then_inc(gate_bias_clear, 1)
            pool.memset(neg_half[:, :], -0.5).then_inc(consts, 1)
            pool.memset(ones[:, :], 1.0).then_inc(consts, 1)
            step.do(pool.memset(ident[:, :], 0.0))
            pool.affine_select(out=ident[:, :], in_=ident[:, :], compare_op=ALU.not_equal, fill=1.0, base=0,
                               pattern=[[-1, P]], channel_multiplier=1).then_inc(consts, 1)
            step.do(pool.memset(pick, 0.0))
            pool.affine_select(out=pick, in_=pick, compare_op=ALU.not_equal, fill=1.0, base=0,
                               pattern=[[-1, 4], [0, P]], channel_multiplier=1).then_inc(consts, 1)
            step.do(pool.memset(flip, 0.0))
            pool.affine_select(out=flip, in_=flip, compare_op=ALU.not_equal, fill=1.0, base=1 - P,
                               pattern=[[1, P]], channel_multiplier=1).then_inc(consts, 1)
            pool.memset(strip_row[:, SEQ:STRIP + 1], MASKED).then_inc(strip_row_ready, 1)
            step.do(pool.memset(before[:, :], 1.0))
            pool.affine_select(out=before[:, :], in_=before[:, :], compare_op=ALU.is_gt, fill=0.0, base=0,
                               pattern=[[1, P]], channel_multiplier=-1).then_inc(consts, 1)
            for t in range(NT):
                pool.wait_ge(mean_sq, t + 1)
                pool.tensor_tensor(rstd[:, t:t + 1], ssq[:, t:t + 1], neg_half[:, 0:1],
                                   ALU.pow).then_inc(rstd_ready, 1)
            pool.iota(lanes[:, :], pattern=[[1, N_EXP]], base=0, channel_multiplier=0,
                      allow_small_or_imprecise_dtypes=True).then_inc(row_ids, 1)
            pool.iota(row_id[:, :, :], pattern=[[P * TOP_K, NT], [1, TOP_K]], base=0,
                      channel_multiplier=TOP_K).then_inc(row_ids, 1)
            step.do(pool.memset(y_idx[:, :], NO_ROW))
            pool.dma_start(list_dram.rearrange("(p c) o -> p (c o)", p=P), y_idx[:, :]).then_inc(list_clear, 16)
            pool.wait_ge(qk_done, 4)
            step.do(pool.memset(above, 0.0))
            pool.affine_select(out=above, in_=above, compare_op=ALU.is_ge, fill=1e4, base=0,
                               pattern=[[1, P]], channel_multiplier=-1).then_inc(consts, 1)
            for n in range(NT):
                pool.wait_ge(mean_sq, NT + n + 1)
                pool.tensor_tensor(small[:, 4:8], small[:, 0:4], neg_half[:, 0:4], ALU.pow).then_inc(rstd_ready, 1)
            for n in range(NT):
                pool.wait_ge(mean_sq, 2 * NT + n + 1)
                pool.tensor_tensor(small[:, 4:8], small[:, 0:4], neg_half[:, 0:4], ALU.pow).then_inc(rstd_ready, 1)
            for t in range(NT):
                pool.wait_ge(mean_sq, 3 * NT + t + 1)
                pool.tensor_tensor(rstd[:, t:t + 1], ssq[:, t:t + 1], neg_half[:, 0:1],
                                   ALU.pow).then_inc(rstd_ready, 1)
            for i in range(2):
                pool.wait_ge(h2_out[i], 16 * NT // 2)
            pool.wait_ge(logits_done, NT)
            pool.wait_ge(b_gu_turned, 1)
            pool.iota(val_e, pattern=[[0, ROUNDS], [1, N_EXP]], base=0, channel_multiplier=0,
                      allow_small_or_imprecise_dtypes=True).then_inc(item_iotas, 1)
            pool.iota(val_c, pattern=[[2, ROUNDS], [LISTS, N_EXP]], base=2, channel_multiplier=0,
                      allow_small_or_imprecise_dtypes=True).then_inc(item_iotas, 1)
            pool.iota(order, pattern=[[1, MAX_EXTRA], [0, ROUNDS * N_EXP]], base=1, channel_multiplier=0,
                      allow_small_or_imprecise_dtypes=True).then_inc(item_iotas, 1)
            pool.wait_ge(list_clear, 16)
            pool.wait_ge(where_ready, 1)
            for t in range(NT):
                for c in range(TOP_K):
                    pool.indirect_dma_start(
                        out=list_dram, out_offset=bass.IndirectOffsetOnAxis(ap=where[:, t, c:c + 1], axis=0),
                        in_=row_id[:, t, c:c + 1], in_offset=None).then_inc(list_out, 16)

            last_x, last_y = pool.to_reg(SEQ - 1), pool.to_reg(SEQ * TOP_K - 1)

            def gather(i):
                for b in range(2):
                    pool.indirect_dma_start(
                        out=xg[:, b, :], out_offset=None, in_=h2_dram,
                        in_offset=bass.IndirectOffsetOnAxis(ap=cur_x[:, b:b + 1], axis=0),
                        bounds_check=last_x, oob_is_err=False).then_inc(xg_in, 16)

            pool.wait_ge(moe_clear, 1)
            pool.wait_ge(cur_x_ready, 1)
            gather(0)
            pool.wait_ge(items_ready, 1)
            last = pool.value_load(n_items[0:1, 0:1], min_val=N_EXP, max_val=ITEMS)
            with pool.Fori(0, ITEMS) as i:
                with pool.If(i < last):
                    pool.wait_ge(cur_x_ready, i + 2)
                    pool.wait_ge(xT_ps, 4 * i + 4)
                    pool.sem_inc(pool_waited, 1)
                    gather(i + 1)
                    pool.wait_ge(cur_y_ready, i + 1)
                    pool.wait_ge(y_evac, 4 * i + 5)
                    pool.sem_inc(pool_waited, 1)
                    for b in range(2):
                        pool.indirect_dma_start(
                            out=y_dram, out_offset=bass.IndirectOffsetOnAxis(ap=cur_y[:, b:b + 1], axis=0),
                            in_=y_rows[:, b, :], in_offset=None,
                            bounds_check=last_y, oob_is_err=False).then_inc(y_out, 16)
                    pool.wait_ge(y_out, 32 * i + 32)
                    pool.sem_inc(y_sent, 1)
            for t in range(NT):
                pool.wait_ge(mean_sq, 4 * NT + t + 1)
                pool.tensor_tensor(rstd[:, t:t + 1], ssq[:, t:t + 1], neg_half[:, 0:1],
                                   ALU.pow).then_inc(rstd_ready, 1)
            pool.wait_ge(xg_in, 32 * last + 32)

        @block.tensor
        def _(pe):
            pe.wait_ge(consts, 7)
            pe.wait_ge(small_in, 16 * N_SMALL)
            pe.transpose(bank(0)[:, 0:V_ROWS], vec_rows, ident[0:V_ROWS, 0:V_ROWS]).then_inc(vec_ps, 1)
            for half in range(2):
                pe.matmul(bank(1 + half)[0:DAH, :], table[:, :], one_hot[:, HALF * half:HALF * half + HALF],
                          start=True, stop=True).then_inc(strip_ps, 1)

            def turn_x(t):
                pe.wait_ge(x_scaled, t + 1)
                if t >= 2:
                    pe.wait_ge(hT_ready, t - 1)
                for k in range(KD):
                    ins = pe.transpose(bank(4 + 2 * (t % 2) + k // 4)[:, P * (k % 4):P * (k % 4) + P],
                                       x_raw[:, t, P * k:P * k + P], ident[:, :])
                ins.then_inc(x_turned, 1)

            def project(o):
                kind, a, b = outs[o]
                if kind < 6:
                    pe.wait_ge(group_in[kind], 16)
                if kind in (QKM, Q, K, MO, GATE):
                    pe.wait_ge(hT_ready, 4 * a + 4)
                if o >= 4:
                    pe.wait_ge(proj_evac, o - 3)
                elif o == 0:
                    pe.wait_ge(vec_ready, 1)
                else:
                    pe.wait_ge(strip_row_ready, 3)
                for k in range(KD):
                    if kind in (V, MV):
                        ps, lhs, rhs = bank(o % 4), hT[:, k, P * b:P * b + P], group_w[kind][:, k, :]
                    elif kind == GATE:
                        ps, lhs, rhs = bank(o % 4)[0:36, :], gate_w[:, k, :], hT[:, k, HALF * a:HALF * a + HALF]
                    else:
                        ps, lhs = bank(o % 4), group_w[kind][:, k, P * b:P * b + P]
                        rhs = hT[:, k, HALF * a:HALF * a + HALF]
                    ins = pe.matmul(ps, lhs, rhs, start=(k == 0), stop=(k == KD - 1))
                ins.then_inc(proj_done, 1)

            for t in range(4):
                turn_x(t)
            for o in range(4):
                project(o)
            for t in range(4, NT):
                turn_x(t)
            for o in range(4, after_group[K]):
                project(o)
            pe.wait_ge(em_ready, 1)
            for n, row in enumerate((row_c, row_b)):
                for t in range(NT):
                    ins = pe.transpose(bank(4)[:, 32 * n + 4 * t:32 * n + 4 * t + 4], row[:, P * t:P * t + P],
                                       ident[0:MLH, 0:MLH])
            ins.then_inc(cols_ps, 1)
            for h in range(MLH):
                for half in range(2):
                    n = 2 * h + half
                    if n >= 2:
                        pe.wait_ge(wide_ready, n - 1)
                    pe.matmul(bank(6 + n % 2), pick[0:MLH, h, :], row_a[:, HALF * half:HALF * half + HALF],
                              start=True, stop=True).then_inc(wide_ps, 1)
            for o in range(after_group[K], N_OUTS):
                project(o)

            pe.wait_ge(strip_in, 16)
            for n in range(8):
                if n >= 2:
                    pe.wait_ge(strip_ready, n - 1)
                pe.matmul(bank(6 + n % 2), flip, strip[:, n // 2, HALF * (n % 2):HALF * (n % 2) + HALF],
                          start=True, stop=True).then_inc(strip_flipped, 1)

            def ml_scores(u):
                t, h, js = ml_units[u]
                pe.wait_ge(ml_w_ready, u - 1) if u >= 2 else None
                lo = 64 * (h % 2)
                for n, j in enumerate(js):
                    ins = pe.matmul(bank(u % 2)[:, P * n:P * n + P], ml_qk[lo:lo + 64, 2 + h // 2, P * j:P * j + P],
                                    ml_qk[lo:lo + 64, h // 2, P * t:P * t + P], start=True, stop=True)
                ins.then_inc(ml_s_done, 1)

            def ml_sums(u):
                t, h, js = ml_units[u]
                pe.wait_ge(ml_w_ready, u + 1)
                if h == 0 and js[0] == 0 and t >= 2:
                    pe.wait_ge(ml_h_read, t - 1)
                for n, j in enumerate(js):
                    c = (DV + 1) * (h % 2)
                    ins = pe.matmul(bank(2 + 2 * (t % 2) + h // 2)[:, c:c + DV + 1], ml_w[:, u % 2, P * n:P * n + P],
                                    ml_v[:, j, h, :], start=(j == 0), stop=(j == t))
                ins.then_inc(ml_h_done, 1)

            def ml_turn(t):
                pe.wait_ge(ml_norm_ready, t + 1)
                pe.wait_ge(ml_mixed, t) if t else None
                for h in range(MLH):
                    ins = pe.transpose(bank(7)[:, P * h:P * h + P], ml_hr[:, h, :], ident[:, :])
                ins.then_inc(ml_turned, 1)

            pe.wait_ge(qk_done, 4)
            pe.wait_ge(proj_evac, N_OUTS)
            pe.wait_ge(v_ones, 1)
            ml_scores(0)
            for u in range(len(ml_units)):
                if u + 1 < len(ml_units):
                    ml_scores(u + 1)
                ml_sums(u)
                for t in range(NT - 1):
                    if u == ml_tile_end[t] + 1:
                        ml_turn(t)
            ml_turn(NT - 1)

            turned = [0]

            def da_logit(u):
                t, h = da_units[u]
                for m in range(2):
                    if u:
                        pe.wait_ge(da_max, 2 * u - 1 + m)
                    for c in range(0, t + 1, 4):
                        w = P * min(4, t + 1 - c)
                        ins = pe.matmul(bank(2 * m + c // 4)[:, 0:w], da_q[64 * m:64 * m + 64, h, P * t:P * t + P],
                                        da_k[64 * m:64 * m + 64, h, P * c:P * c + w], start=True, stop=True)
                    ins.then_inc(da_logits, 1)

            def da_values(u):
                t, h = da_units[u]
                pe.wait_ge(da_a_ready, u + 1)
                first = turned[0]
                for n, js in enumerate(da_groups[u]):
                    g = first + n
                    if g >= 2:
                        pe.wait_ge(da_aT_ready, g - 1)
                    for i, j in enumerate(js):
                        ins = pe.transpose(bank(4 + g % 2)[:, P * i:P * i + P], prob[u % 2][0][:, P * j:P * j + P],
                                           ident[:, :])
                    ins.then_inc(da_aT_ps, 1)
                if h == 0 and t >= 1:
                    pe.wait_ge(da_o_read, t)
                for n, js in enumerate(da_groups[u]):
                    g = first + n
                    pe.wait_ge(da_aT_ready, g + 1)
                    for i, j in enumerate(js):
                        ins = pe.matmul(bank(6)[:, P * h:P * h + P], probT[:, g % 2, P * i:P * i + P],
                                        da_v[:, j, P * h:P * h + P], start=(j == 0), stop=(j == t))
                ins.then_inc(da_o_done, 1)
                turned[0] += len(da_groups[u])

            def da_turn(t):
                pe.wait_ge(da_norm_ready, t + 1)
                pe.wait_ge(ml_mixed, NT)
                if t:
                    pe.wait_ge(da_mixed, t)
                for h in range(DAH):
                    ins = pe.transpose(bank(7)[:, P * h:P * h + P], da_o[:, h, :], ident[:, :])
                ins.then_inc(da_turned, 1)

            pe.wait_ge(ml_h_read, NT)
            da_logit(0)
            for u in range(len(da_units)):
                if u + 1 < len(da_units):
                    da_logit(u + 1)
                da_values(u)
                if u % DAH == 1 and u > DAH:
                    da_turn(u // DAH - 1)
            da_turn(NT - 1)

            def out_project(t):
                if t == 0:
                    pe.wait_ge(w_out_in0, 16)
                    pe.wait_ge(w_out_in1, 16)
                    pe.wait_ge(da_mixed, NT)
                if t >= 2:
                    pe.wait_ge(x1_ready, t - 1)
                for half in range(2):
                    for k in range(KD):
                        ins = pe.matmul(bank(2 * (t % 2) + half), mixT[:, k, P * t:P * t + P],
                                        w_o[k // 4][:, k % 4, HALF * half:HALF * half + HALF],
                                        start=(k == 0), stop=(k == KD - 1))
                ins.then_inc(out_proj_done, 1)

            out_project(0)
            for t in range(NT):
                if t + 1 < NT:
                    out_project(t + 1)
                pe.wait_ge(h2_ready, t + 1)
                if t:
                    pe.wait_ge(h2T_ready, 2 * t)
                for k in range(KD):
                    ins = pe.transpose(bank(4 + k // 4)[:, P * (k % 4):P * (k % 4) + P],
                                       h2[:, t % 2, P * k:P * k + P], ident[:, :])
                    if k % 4 == 3:
                        ins.then_inc(h2_turned, 1)
                pe.wait_ge(h2T_ready, 2 * t + 2)
                if t:
                    pe.wait_ge(top_ready, t)
                for k in range(KD):
                    ins = pe.matmul(bank(6)[:, 0:N_EXP], h2T[t % 2][:, k, :], rw[:, k, :],
                                    start=(k == 0), stop=(k == KD - 1))
                ins.then_inc(logits_done, 1)
            pe.wait_ge(b_gu_in, 16)
            pe.wait_ge(x1_ready, NT)
            for f in range(2 * NF):
                ins = pe.transpose(bank(0)[:, 32 * f:32 * f + 32], b_gu_rows[:, P * f:P * f + P],
                                   ident[0:N_EXP, 0:N_EXP])
            ins.then_inc(b_gu_turned, 1)
            pe.wait_ge(chosen_ready, NT)
            for t in range(NT):
                for s in range(t + 1):
                    pe.matmul(bank(7)[:, 32 * t:32 * t + 32], (before if s == t else ones)[:, :], mask[:, s, :],
                              start=(s == 0), stop=(s == t))
            for s in range(NT):
                ins = pe.matmul(bank(7)[:, 256:288], ones[:, :], mask[:, s, :], start=(s == 0), stop=(s == NT - 1))
            ins.then_inc(pos_ps, 1)
            for t in range(NT):
                ins = pe.transpose(bank(4 + t // 4)[0:N_EXP, P * (t % 4):P * (t % 4) + P], g_all[:, t, :],
                                   ident[:, :])
            ins.then_inc(g_turned, 1)
            pe.wait_ge(g_allT_ready, 2)
            pe.wait_ge(b_down_in, 16)
            pe.wait_ge(b_gu_ready, 1)
            for t in range(NT):
                if t >= 2:
                    pe.wait_ge(x1_full, t - 1)
                for half in range(2):
                    ins = pe.matmul(bank(2 * (t % 2) + half), g_allT[:, t, :],
                                    b_down[:, HALF * half:HALF * half + HALF], start=True, stop=True)
                ins.then_inc(down_bias_done, 1)

            def turn_rows(i):
                pe.wait_ge(xg_in, 32 * i + 32)
                for q in range(4):
                    for k in range(2):
                        for b in range(2):
                            ins = pe.transpose(bank(2 + q)[:, 256 * k + P * b:256 * k + P * b + P],
                                               xg[:, b, P * (2 * q + k):P * (2 * q + k) + P], ident[:, :])
                    ins.then_inc(xT_ps, 1)

            def by_width(n, widths, body):
                if len(widths) == 1:
                    body(widths[0])
                    return
                mid = len(widths) // 2
                with pe.If(n <= widths[mid - 1]):
                    by_width(n, widths[:mid], body)
                with pe.Else():
                    by_width(n, widths[mid:], body)

            pe.wait_ge(x1_full, NT)
            turn_rows(0)
            pe.sem_inc(yT_ps, 1)
            pe.sem_inc(y_ps, 1)
            pe.wait_ge(items_ready, 1)
            last = pe.value_load(n_items[0:1, 0:1], min_val=N_EXP, max_val=ITEMS)
            n_next = pe.alloc_register("n_next")
            pe.load(n_next, item_n[0:1, 0:1])
            with pe.Fori(0, ITEMS) as i:
                with pe.If(i < last):
                    n = pe.snap(n_next, min_val=0, max_val=SEQ)
                    pe.wait_ge(xT_evac, 4 * i + 4)

                    def gate_up(w):
                        for j in range(NF):
                            if j % 2 == 0:
                                pe.wait_ge(gu_in[j // 2], 32 * i + 32)
                            pe.wait_ge(glu_read, 8 * i + j + 1)
                            for h in range(2):
                                for k in range(KD):
                                    ins = pe.matmul(bank(j % 2)[:, 256 * h:256 * h + w],
                                                    gu_w[j // 2][:, h, k, P * (j % 2):P * (j % 2) + P],
                                                    xT[:, k, 0:w], start=(k == 0), stop=(k == KD - 1))
                            ins.then_inc(gu_done, 1)

                    def down(w):
                        pe.wait_ge(act_ready, 8 * i + 2 + NF - 2)
                        for m in range(KD):
                            if m % 2 == 0:
                                pe.wait_ge(down_in[m // 2], 16 * i + 16)
                            pe.wait_ge(yT_evac, 8 * i + m + 1)
                            for k in range(NF):
                                if m == 0 and k >= NF - 2:
                                    pe.wait_ge(act_ready, 8 * i + 2 + k + 1)
                                ins = pe.matmul(bank(6 + m % 2)[:, 0:w],
                                                down_w[m // 2][:, k, P * (m % 2):P * (m % 2) + P],
                                                actT[:, k, 0:w], start=(k == 0), stop=(k == NF - 1))
                            ins.then_inc(yT_ps, 1)

                    def item(w):
                        gate_up(w)
                        pe.wait_ge(y_evac, 4 * i + 1)
                        turn_rows(i + 1)
                        down(w)

                    by_width(n, WIDTHS, item)
                    pe.load(n_next, item_n[0:1, bass.ds(i + 1, 1)])
                    pe.wait_ge(xT_evac, 4 * i + 8)
                    for q in range(4):
                        pe.wait_ge(yT_evac, 8 * i + 6 + 4 * (q % 2))
                        for m in range(4):
                            ins = pe.transpose(bank(2 + q)[:, P * m:P * m + P],
                                               yT[:, 4 * (q % 2) + m, P * (q // 2):P * (q // 2) + P], ident[:, :])
                        ins.then_inc(y_ps, 1)

        @block.scalar
        def _(act):
            step = Steps(act, act_step)
            for ap, row, n in ((norm_attn_g, V_GA, 8), (norm_ffn_g, V_GF, 8), (diff_norm_g, V_GD, 4),
                               (mlstm_norm_g, V_GM, 4), (mlstm_conv_b, V_CB, 4), (mlstm_o_b, V_OB, 4)):
                act.dma_start(vec_rows[row:row + n, :], ap.rearrange("l (k p) -> (l k) p", p=P)).then_inc(small_in, 16)
            act.dma_start(vec_rows[V_CW:V_CW + 16, :], mlstm_conv_w.rearrange("l c (k p) -> (l c k) p", p=P)) \
               .then_inc(small_in, 16)
            act.wait_ge(gate_bias_clear, 1)
            act.dma_start(gate_bias[0:4, :], mlstm_gate_b[:, 0:4].rearrange("l (g o) -> (l g) o", o=1)) \
               .then_inc(small_in, 16)
            act.dma_start(gate_bias[32:36, :], mlstm_gate_b[:, 4:8].rearrange("l (g o) -> (l g) o", o=1)) \
               .then_inc(small_in, 16)
            act.dma_start(table[:, :], rel_bias_table).then_inc(small_in, 16)
            act.dma_start(one_hot, buckets).then_inc(small_in, 16)
            for n, v in enumerate((lambda_q1, lambda_k1, lambda_q2, lambda_k2)):
                act.dma_start(lam_in[:, n, :], v.rearrange("l d -> (l d)").partition_broadcast(P)).then_inc(small_in, 16)
            act.dma_start(rb_wide[:, :], router_b.rearrange("l d -> (l d)").partition_broadcast(P)).then_inc(small_in, 16)
            act.dma_start(rw[:, :, :], router_w.rearrange("l (k p) e -> p (l k) e", p=P)).then_inc(small_in, 16)
            act.wait_ge(consts, 1)
            for lo, c in ((0, 3072), (32, 3076)):
                act.dma_start(gate_w[:, :, lo:lo + 4], w_in_k[:, :, c:c + 4]).then_inc(small_in, 16)
            act.wait_ge(strip_ps, 2)
            for half in range(2):
                act.activation(strip_row[:, HALF * half:HALF * half + HALF], bank(1 + half)[0:DAH, :],
                               ACT.Copy).then_inc(strip_row_ready, 1)

            for o, (kind, a, b) in enumerate(outs):
                act.wait_ge(proj_done, o + 1)
                if o == 0:
                    act.wait_ge(vec_ready, 1)
                cols = slice(HALF * a, HALF * a + HALF)
                if kind == QKM:
                    ins = act.activation(ml_raw[:, b, cols], bank(o % 4), ACT.Copy)
                elif kind == GATE:
                    ins = act.activation(gate_rows[0:36, cols], bank(o % 4)[0:36, :], ACT.Identity,
                                         bias=gate_bias[0:36, :])
                elif kind == Q:
                    if (a, b) == (0, 0):
                        act.wait_ge(strip_out, 16)
                    ins = act.activation(da_q[:, b, cols], bank(o % 4), ACT.Copy, scale=DQ ** -0.5)
                elif kind == K:
                    ins = act.activation(da_k[:, b, cols], bank(o % 4), ACT.Copy)
                elif kind == V:
                    if b == 0:
                        act.wait_ge(cols_ready, 2)
                        act.wait_ge(wide_ready, 8)
                    ins = act.activation(da_v[:, b, :], bank(o % 4), ACT.Copy)
                elif kind == MV:
                    ins = act.activation(ml_v[:, b, :, 0:DV], kn(bank(o % 4), MLH), ACT.Copy)
                else:
                    ins = act.activation(o_gate[:, b, cols], bank(o % 4), ACT.Sigmoid,
                                         bias=vec[:, V_OB + b:V_OB + b + 1])
                ins.then_inc(proj_evac, 1)
                if o + 1 == after_group[GATE]:
                    act.wait_ge(proj_evac, o + 1)
                    step.do(act.activation(row_a, gate_rows[32:36, :], ACT.Abs))
                    step.do(act.activation(row_a, row_a, ACT.Exp, scale=-1.0))
                    act.activation(row_a, row_a, ACT.Ln, bias=ones[0:MLH, 0:1]).then_inc(log_f_part, 1)
                if o + 1 == after_group[Q]:
                    for m in range(4):
                        act.wait_ge(conv_done, m + 1)
                        act.activation(ml_sig[:, m, :], ml_qk[:, m, :], ACT.Sigmoid).then_inc(sig_done, 1)
                if o + 1 == after_group[K]:
                    act.wait_ge(em_in, 1)
                    act.activation(row_b, row_b, ACT.Exp, scale=-1.0).then_inc(em_ready, 1)
                    act.wait_ge(qk_done, 4)
                    for n in range(8):
                        act.wait_ge(wide_ps, n + 1)
                        act.activation(m_wide[:, n // 2, HALF * (n % 2):HALF * (n % 2) + HALF], bank(6 + n % 2),
                                       ACT.Copy).then_inc(wide_ready, 1)

            for n in range(8):
                act.wait_ge(strip_flipped, n + 1)
                act.activation(strip[:, n // 2, HALF * (n % 2):HALF * (n % 2) + HALF], bank(6 + n % 2),
                               ACT.Copy).then_inc(strip_ready, 1)
            act.wait_ge(lam_ready, 1)
            act.activation(lam[:, 2:4], lam[:, 0:2], ACT.Exp).then_inc(lam_exp, 1)

            for u, (t, h, js) in enumerate(ml_units):
                if u >= 2:
                    act.wait_ge(ml_w_ready, u - 1)
                for n, j in enumerate(js):
                    if j == t:
                        act.wait_ge(ml_e_ready, MLH * t + h + 1)
                        src, bias = ml_e[:, (MLH * t + h) % 2, :], 0.0
                        ins = act.activation(ml_decay[:, u % 2, P * n:P * n + P], src, ACT.Exp, scale=-1.0)
                    else:
                        ins = act.activation(ml_decay[:, u % 2, P * n:P * n + P], m_wide[:, h, P * t:P * t + P],
                                             ACT.Exp, bias=a_col[:, j, h:h + 1], scale=-1.0)
                ins.then_inc(ml_d_ready, 1)

            def da_exps(u):
                t, h = da_units[u]
                w = P * (t + 1)
                for m in range(2):
                    act.wait_ge(da_max, 2 * u + m + 1)
                    p = prob[u % 2][m][:, 0:w]
                    act.activation(p, p, ACT.Exp, bias=small[:, 8 + 4 * (u % 2) + m:9 + 4 * (u % 2) + m],
                                   accum_out=small[:, 10 + 4 * (u % 2) + m:11 + 4 * (u % 2) + m]).then_inc(da_exp, 1)

            g = 0
            da_exps(0)
            for u in range(len(da_units)):
                if u + 1 < len(da_units):
                    da_exps(u + 1)
                for js in da_groups[u]:
                    act.wait_ge(da_aT_ps, g + 1)
                    w = P * len(js)
                    act.activation(probT[:, g % 2, 0:w], bank(4 + g % 2)[:, 0:w], ACT.Copy).then_inc(da_aT_ready, 1)
                    g += 1
            for t in range(NT):
                act.wait_ge(top_ready, t + 1)
                act.activation(gate[:, t, :], top8[:, 0:TOP_K], ACT.Exp, bias=small[:, 16:17],
                               accum_out=small[:, 17:18]).then_inc(gate_exp, 1)

            act.sem_inc(yT_evac, 2)
            act.sem_inc(y_evac, 1)
            act.sem_inc(lin_read, 2)
            act.sem_inc(y_sent, 1)
            act.wait_ge(items_ready, 1)
            last = act.value_load(n_items[0:1, 0:1], min_val=N_EXP, max_val=ITEMS)
            with act.Fori(0, ITEMS) as i:
                with act.If(i < last):
                    act.wait_ge(cur_b_ready, i + 1)
                    for j in range(NF):
                        act.wait_ge(gu_done, 8 * i + j + 1)
                        act.wait_ge(act_ready, 8 * i + j + 1)
                        act.activation(lin_b[:, j % 2, :], bank(j % 2)[:, 256:512], ACT.Identity,
                                       bias=cur_b[:, NF + j:NF + j + 1]).then_inc(lin_read, 1)
                        act.wait_ge(glu_read, 8 * i + j + 3)
                        act.activation(glu_s[:, j % 2, :], glu_t[:, j % 2, :], ACT.Sigmoid,
                                       scale=ALPHA).then_inc(sig_ready, 1)
                    act.wait_ge(y_ps, 4 * i + 1)
                    for m in range(KD):
                        act.wait_ge(yT_ps, 8 * i + m + 2)
                        act.activation(yT[:, m, :], bank(6 + m % 2)[:, 0:ITEM], ACT.Copy).then_inc(yT_evac, 1)
                    act.wait_ge(y_sent, i + 1)
                    for q in range(4):
                        act.wait_ge(y_ps, 4 * i + q + 2)
                        act.activation(y_rows[:, q // 2, HALF * (q % 2):HALF * (q % 2) + HALF], bank(2 + q),
                                       ACT.Copy).then_inc(y_evac, 1)

        @block.vector
        def _(dve):
            step = Steps(dve, dve_step)
            junk = unit11[:, 2560:3584]

            def square_sum(t, src):
                step.do(dve.tensor_tensor_reduce(junk, src[:, t, :], src[:, t, :],
                                                 1.0, 0.0, ALU.mult, ALU.add, ssq[:, t:t + 1]))
                dve.tensor_scalar(ssq[:, t:t + 1], ssq[:, t:t + 1], 1.0 / D, EPS, ALU.mult, ALU.add).then_inc(mean_sq, 1)

            dve.wait_ge(x_in[0], 16)
            square_sum(0, x_raw)
            for t in range(NT):
                if t + 1 < NT:
                    dve.wait_ge(x_in[t + 1], 16)
                    square_sum(t + 1, x_raw)
                dve.wait_ge(rstd_ready, t + 1)
                dve.tensor_scalar(x_raw[:, t, :], x_raw[:, t, :], rstd[:, t:t + 1], None, ALU.mult).then_inc(x_scaled, 1)
                if t == 0:
                    dve.wait_ge(vec_ps, 1)
                    dve.tensor_copy(vec[:, :], bank(0)[:, 0:V_ROWS]).then_inc(vec_ready, 1)
                    dve.wait_ge(vec_ready, 1)
                dve.wait_ge(x_turned, t + 1)
                for kb in range(2):
                    ins = dve.tensor_tensor(hT[:, 4 * kb:4 * kb + 4, P * t:P * t + P],
                                            kn(bank(4 + 2 * (t % 2) + kb), 4),
                                            wide(vec[:, V_GA + 4 * kb:V_GA + 4 * kb + 4], P), ALU.mult)
                ins.then_inc(hT_ready, 1)

            dve.wait_ge(small_in, 16 * N_SMALL)
            for n in range(2):
                step.do(dve.tensor_tensor_reduce(lam_in[:, 2 * n, :], lam_in[:, 2 * n, :], lam_in[:, 2 * n + 1, :], 1.0, 0.0,
                                                 ALU.mult, ALU.add, lam[:, n:n + 1]))
            dve.tensor_scalar(gd_scaled[:, :], vec[:, V_GD:V_GD + 4], 1.0 - LAM_INIT, None,
                              ALU.mult).then_inc(lam_ready, 1)

            dve.wait_ge(log_f_part, 1)
            step.do(dve.tensor_scalar(row_b, gate_rows[32:36, :], 0.0, None, ALU.min))
            step.do(dve.tensor_tensor(row_b, row_b, row_a, ALU.subtract))

            def running(src, dst, op):
                s = 1
                while s < SEQ:
                    dve.tensor_tensor(dst[:, s:], src[:, s:], src[:, :SEQ - s], op)
                    step.do(dve.tensor_copy(dst[:, 0:s], src[:, 0:s]))
                    src, dst = dst, src
                    s *= 2

            running(row_b, row_a, ALU.add)
            step.do(dve.tensor_tensor(row_c, row_g, row_b, ALU.subtract))
            step.do(dve.tensor_scalar(row_a, row_c, 0.0, None, ALU.max))
            running(row_a, row_g, ALU.max)
            dve.tensor_tensor(row_b, row_b, row_a, ALU.add).then_inc(em_in, 1)
            dve.wait_ge(proj_evac, after_group[GATE])
            for m in range(4):
                def tap(n):
                    return vec[:, V_CW + 4 * n + m:V_CW + 4 * n + m + 1]
                step.do(dve.tensor_scalar(ml_qk[:, m, :], ml_raw[:, m, :], tap(3), vec[:, V_CB + m:V_CB + m + 1],
                                          ALU.mult, ALU.add))
                for s in range(1, 4):
                    ins = dve.scalar_tensor_tensor(out=ml_qk[:, m, s:], in0=ml_raw[:, m, :SEQ - s], scalar=tap(3 - s),
                                                   in1=ml_qk[:, m, s:], op0=ALU.mult, op1=ALU.add)
                    if s < 3:
                        step.do(ins)
                    else:
                        ins.then_inc(conv_done, 1)
            for m in range(4):
                dve.wait_ge(sig_done, m + 1)
                dve.scalar_tensor_tensor(out=ml_qk[:, m, :], in0=ml_qk[:, m, :], scalar=1.0 if m < 2 else DQ ** -0.5,
                                         in1=ml_sig[:, m, :], op0=ALU.mult, op1=ALU.mult).then_inc(qk_done, 1)
            dve.wait_ge(cols_ps, 1)
            dve.tensor_copy(a_col[:, :, :], kn(bank(4)[:, 0:32])).then_inc(cols_ready, 1)
            dve.tensor_copy(em_col[:, :, :], kn(bank(4)[:, 32:64])).then_inc(cols_ready, 1)
            dve.wait_ge(proj_evac, N_OUTS)
            dve.memset(ml_v[:, :, :, DV:DV + 1], 1.0).then_inc(v_ones, 1)
            step.do(dve.tensor_tensor(o_gate, o_gate, wide(vec[:, V_GM:V_GM + 4], SEQ), ALU.mult))
            dve.wait_ge(lam_exp, 1)
            step.do(dve.tensor_tensor(lam[:, 0:1], lam[:, 3:4], lam[:, 2:3], ALU.subtract))
            step.do(dve.tensor_scalar(lam[:, 1:2], lam[:, 0:1], -LAM_INIT, None, ALU.add))

            def head_mean_square(src, sq):
                step.do(dve.tensor_tensor(sq, src, src, ALU.mult))
                step.do(dve.tensor_reduce(small[:, 0:4], sq, AX, ALU.add))
                dve.tensor_scalar(small[:, 0:4], small[:, 0:4], 1.0 / DV, EPS, ALU.mult, ALU.add).then_inc(mean_sq, 1)

            def ml_finish(t):
                dve.wait_ge(ml_h_done, ml_tile_end[t])
                for b in range(2):
                    ins = dve.tensor_copy(ml_h[:, 2 * b:2 * b + 2, :],
                                          bank(2 + 2 * (t % 2) + b)[:, 0:2 * (DV + 1)].rearrange("p (h d) -> p h d", h=2))
                ins.then_inc(ml_h_read, 1)
                dve.wait_ge(ml_h_read, t + 1)
                step.do(dve.scalar_tensor_tensor(out=small[:, 20:24], in0=ml_h[:, :, DV], scalar=-1.0,
                                                 in1=ml_h[:, :, DV], op0=ALU.mult, op1=ALU.max))
                step.do(dve.tensor_tensor(small[:, 20:24], small[:, 20:24], em_col[:, t, :], ALU.max))
                step.do(dve.reciprocal(small[:, 24:28], small[:, 20:24]))
                dve.wait_ge(ml_turned, t) if t else None
                step.do(dve.tensor_tensor(ml_hr, ml_h[:, :, 0:DV], wide(small[:, 24:28], DV), ALU.mult))
                head_mean_square(ml_hr, ml_sq)
                dve.wait_ge(rstd_ready, NT + t + 1)
                dve.tensor_tensor(ml_hr, ml_hr, wide(small[:, 4:8], DV), ALU.mult).then_inc(ml_norm_ready, 1)

            def ml_mix(t):
                dve.wait_ge(ml_turned, t + 1)
                dve.tensor_tensor(mixT[:, 4:8, P * t:P * t + P], kn(bank(7), 4), o_gate[:, :, P * t:P * t + P],
                                  ALU.mult).then_inc(ml_mixed, 1)

            for u, (t, h, js) in enumerate(ml_units):
                if js[-1] == t:
                    dve.wait_ge(consts, 8)
                    n = MLH * t + h
                    if n >= 2:
                        dve.wait_ge(ml_d_ready, u - 1)
                    dve.scalar_tensor_tensor(out=ml_e[:, n % 2, :], in0=m_wide[:, h, P * t:P * t + P],
                                             scalar=a_col[:, t, h:h + 1], in1=above, op0=ALU.subtract,
                                             op1=ALU.max).then_inc(ml_e_ready, 1)
                dve.wait_ge(ml_s_done, u + 1)
                dve.wait_ge(ml_d_ready, u + 1)
                if u >= 2:
                    dve.wait_ge(ml_h_done, u - 1)
                w = P * len(js)
                dve.tensor_tensor(ml_w[:, u % 2, 0:w], bank(u % 2)[:, 0:w], ml_decay[:, u % 2, 0:w],
                                  ALU.mult).then_inc(ml_w_ready, 1)
                for n in range(NT - 1):
                    if u == ml_tile_end[n]:
                        ml_finish(n)
                    if u == ml_tile_end[n] + 2:
                        ml_mix(n)
            ml_finish(NT - 1)
            ml_mix(NT - 1)

            def da_softmax_in(u):
                t, h = da_units[u]
                w = P * (t + 1)
                s = 8 + 4 * (u % 2)
                if u == 0:
                    dve.wait_ge(strip_ready, 8)
                if u >= 2:
                    dve.wait_ge(da_aT_ps, sum(len(x) for x in da_groups[:u - 1]))
                for m in range(2):
                    dve.wait_ge(da_logits, 2 * u + m + 1)
                    step.do(dve.tensor_tensor_reduce(prob[u % 2][m][:, 0:w], banks2(2 * m)[:, 0:w],
                                                     strip[:, h, SEQ - w:SEQ], 1.0, 3 * MASKED, ALU.add, ALU.max,
                                                     small[:, 28 + m:29 + m]))
                    dve.tensor_scalar(small[:, s + m:s + m + 1], small[:, 28 + m:29 + m], -1.0, None,
                                      ALU.mult).then_inc(da_max, 1)

            def da_combine(u):
                t, h = da_units[u]
                w = P * (t + 1)
                s = 8 + 4 * (u % 2)
                dve.wait_ge(da_exp, 2 * u + 2)
                if u:
                    dve.wait_ge(da_a_ready, u)
                step.do(dve.reciprocal(small[:, 20:22], small[:, s + 2:s + 4]))
                step.do(dve.tensor_tensor(small[:, 22:23], small[:, 21:22], lam[:, 1:2], ALU.mult))
                p0, p1 = prob[u % 2][0][:, 0:w], prob[u % 2][1][:, 0:w]
                step.do(dve.tensor_scalar(p1, p1, small[:, 22:23], None, ALU.mult))
                dve.scalar_tensor_tensor(out=p0, in0=p0, scalar=small[:, 20:21], in1=p1, op0=ALU.mult,
                                         op1=ALU.add).then_inc(da_a_ready, 1)

            def da_finish(t):
                dve.wait_ge(da_o_done, DAH * t + DAH)
                if t:
                    dve.wait_ge(da_turned, t)
                dve.tensor_copy(da_o, kn(bank(6), DAH)).then_inc(da_o_read, 1)
                dve.wait_ge(da_o_read, t + 1)
                head_mean_square(da_o, da_sq)
                dve.wait_ge(rstd_ready, 2 * NT + t + 1)
                dve.tensor_tensor(da_o, da_o, wide(small[:, 4:8], DV), ALU.mult).then_inc(da_norm_ready, 1)

            def da_mix(t):
                dve.wait_ge(da_turned, t + 1)
                dve.tensor_tensor(mixT[:, 0:4, P * t:P * t + P], kn(bank(7), 4), wide(gd_scaled[:, :], P),
                                  ALU.mult).then_inc(da_mixed, 1)

            da_softmax_in(0)
            for u in range(len(da_units)):
                if u + 1 < len(da_units):
                    da_softmax_in(u + 1)
                da_combine(u)
                if u % DAH == 0 and u:
                    da_finish(u // DAH - 1)
                if u % DAH == 2 and u > DAH:
                    da_mix(u // DAH - 1)
            da_finish(NT - 1)
            da_mix(NT - 1)

            def residual(t):
                dve.wait_ge(out_proj_done, t + 1)
                dve.wait_ge(x_again_in[t % 2], 16 * (t // 2 + 1))
                dve.tensor_tensor(x1[:, t, :], banks2(2 * (t % 2)), x_again[:, t % 2, :], ALU.add).then_inc(x1_ready, 1)
                dve.wait_ge(x1_ready, t + 1)
                if t >= 2:
                    dve.wait_ge(h2_out[t % 2], 16 * (t // 2))
                step.do(dve.tensor_tensor_reduce(h2[:, t % 2, :], x1[:, t, :], x1[:, t, :], 1.0, 0.0, ALU.mult, ALU.add,
                                                 ssq[:, t:t + 1]))
                dve.tensor_scalar(ssq[:, t:t + 1], ssq[:, t:t + 1], 1.0 / D, EPS, ALU.mult, ALU.add).then_inc(mean_sq, 1)
                dve.wait_ge(rstd_ready, 3 * NT + t + 1)
                dve.tensor_scalar(h2[:, t % 2, :], x1[:, t, :], rstd[:, t:t + 1], None, ALU.mult).then_inc(h2_ready, 1)
                for kb in range(2):
                    dve.wait_ge(h2_turned, 2 * t + kb + 1)
                    dve.tensor_tensor(h2T[t % 2][:, 4 * kb:4 * kb + 4, :], kn(bank(4 + kb), 4),
                                      wide(vec[:, V_GF + 4 * kb:V_GF + 4 * kb + 4], P), ALU.mult).then_inc(h2T_ready, 1)

            def choose(t):
                dve.wait_ge(logits_done, t + 1)
                if t == 0:
                    dve.wait_ge(row_ids, 2)
                step.do(dve.tensor_tensor(lg[:, :], bank(6)[:, 0:N_EXP], rb_wide[:, :], ALU.add))
                step.do(dve.max(top8[:, :], lg[:, :]))
                step.do(dve.max_index(idx8[:, :], top8[:, :], lg[:, :]))
                step.do(dve.tensor_copy(idxf[:, t, :], idx8[:, 0:TOP_K]))
                dve.tensor_scalar(small[:, 16:17], top8[:, 0:1], -1.0, None, ALU.mult).then_inc(top_ready, 1)
                for c in range(TOP_K):
                    ins = dve.tensor_scalar(chosen[:, t, c, :], lanes[:, :], idxf[:, t, c:c + 1], None, ALU.is_equal)
                step.do(ins)
                step.do(dve.tensor_reduce(mask[:, t, :], chosen[:, t, :, :].rearrange("p c e -> p e c"), AX, ALU.add))
                dve.wait_ge(gate_exp, t + 1)
                step.do(dve.reciprocal(small[:, 18:19], small[:, 17:18]))
                step.do(dve.tensor_scalar(gate[:, t, :], gate[:, t, :], small[:, 18:19], None, ALU.mult))
                step.do(dve.tensor_scalar(g_all[:, t, :], chosen[:, t, 0, :], gate[:, t, 0:1], None, ALU.mult))
                for c in range(1, TOP_K):
                    ins = dve.scalar_tensor_tensor(out=g_all[:, t, :], in0=chosen[:, t, c, :], scalar=gate[:, t, c:c + 1],
                                                   in1=g_all[:, t, :], op0=ALU.mult, op1=ALU.add)
                    if c < TOP_K - 1:
                        step.do(ins)
                ins.then_inc(chosen_ready, 1)

            residual(0)
            for t in range(NT):
                if t + 1 < NT:
                    residual(t + 1)
                choose(t)
            dve.wait_ge(b_gu_turned, 1)
            dve.tensor_copy(b_gu[:, :, :].rearrange("p e f -> p f e"),
                            bank(0).rearrange("p (f e) -> p f e", e=N_EXP)).then_inc(b_gu_ready, 1)
            dve.wait_ge(pos_ps, 1)
            step.do(dve.tensor_copy(counts[:, :], bank(7)[:, 256:288]))
            for t in range(NT):
                step.do(dve.tensor_tensor(chosen[:, t, :, :], chosen[:, t, :, :],
                                          again(bank(7)[:, 32 * t:32 * t + 32], TOP_K), ALU.mult))
                step.do(dve.tensor_reduce(slot[:, t, :], chosen[:, t, :, :], AX, ALU.add))
            step.do(dve.tensor_copy(slot_i[:, :, :], slot[:, :, :]))
            step.do(dve.tensor_scalar(slot_lo[:, :, :], slot_i[:, :, :], P - 1, 8, ALU.bitwise_and, ALU.logical_shift_left))
            step.do(dve.tensor_scalar(slot_i[:, :, :], slot_i[:, :, :], 7, None, ALU.logical_shift_right))
            step.do(dve.tensor_tensor(slot[:, :, :], slot_i[:, :, :], slot_lo[:, :, :], ALU.add))
            dve.scalar_tensor_tensor(out=where[:, :, :], in0=idxf[:, :, :], scalar=float(LISTS), in1=slot[:, :, :],
                                     op0=ALU.mult, op1=ALU.add).then_inc(where_ready, 1)
            dve.wait_ge(g_turned, 1)
            for b in range(2):
                dve.tensor_copy(g_allT[:, 4 * b:4 * b + 4, :], kn(bank(4 + b)[0:N_EXP, :], 4)).then_inc(g_allT_ready, 1)
            for t in range(NT):
                dve.wait_ge(down_bias_done, t + 1)
                dve.tensor_tensor(x1[:, t, :], x1[:, t, :], banks2(2 * (t % 2)), ALU.add).then_inc(x1_full, 1)

            R, N = ROUNDS, ROUNDS * N_EXP
            dve.wait_ge(item_iotas, 3)
            for r in range(R):
                dve.tensor_scalar(flag[:, N_EXP * r:N_EXP * (r + 1)], counts[0:1, :], float(ITEM * (r + 1)), None,
                                  ALU.is_gt)
                ins = dve.tensor_scalar(val_n[:, N_EXP * r:N_EXP * (r + 1)], counts[0:1, :],
                                        float(-ITEM * (r + 1)), None, ALU.add)
            step.do(ins)
            step.do(dve.tensor_copy(pos, flag))
            src, dst, s = pos, pos2, 1
            while s < N:
                dve.tensor_tensor(dst[:, s:], src[:, s:], src[:, :N - s], ALU.add)
                step.do(dve.tensor_copy(dst[:, 0:s], src[:, 0:s]))
                src, dst, s = dst, src, 2 * s
            step.do(dve.tensor_tensor(eq, again(src, MAX_EXTRA), order, ALU.is_equal))
            step.do(dve.tensor_tensor(eq, eq, again(flag, MAX_EXTRA), ALU.mult))
            dve.tensor_copy(item_e[0:1, 0:N_EXP], lanes[0:1, :])
            dve.tensor_scalar(item_col[0:1, 0:N_EXP], lanes[0:1, :], float(LISTS), None, ALU.mult)
            dve.tensor_copy(item_n[0:1, 0:N_EXP], counts[0:1, :])
            for i, (val, tab) in enumerate(((val_e, item_e), (val_c, item_col), (val_n, item_n))):
                step.do(dve.tensor_tensor(pick_v, eq, again(val, MAX_EXTRA), ALU.mult))
                step.do(dve.tensor_reduce(got[:, 16 * i:16 * i + MAX_EXTRA], pick_v, AX, ALU.add))
                dve.tensor_copy(tab[0:1, N_EXP:N_EXP + MAX_EXTRA], got[:, 16 * i:16 * i + MAX_EXTRA])
                dve.memset(tab[0:1, ITEMS:ITEMS + 1], 0)
            dve.tensor_scalar(n_items[:, :], src[:, N - 1:N], float(N_EXP), None, ALU.add).then_inc(items_ready, 1)
            dve.wait_ge(list_in, 16)
            step.do(dve.tensor_scalar(x_idx[:, :], y_idx[:, :], 2, None, ALU.logical_shift_right))
            dve.memset(pairA[:, 0:2048], 0.0)
            dve.memset(PS[:, 0:4, :], 0.0)
            step.do(dve.memset(PS[:, 4:8, :], 0.0))
            dve.sem_inc(moe_clear, 1)

            dve.wait_ge(items_ready, 1)
            last = dve.value_load(n_items[0:1, 0:1], min_val=N_EXP, max_val=ITEMS)
            dve.tensor_copy(cur_x[:, :], x_idx[:, 0:2]).then_inc(cur_x_ready, 1)

            def take_xT(i):
                for q in range(4):
                    dve.wait_ge(xT_ps, 4 * i + q + 1)
                    dve.tensor_tensor(xT[:, 2 * q:2 * q + 2, :], kn(bank(2 + q), 2),
                                      wide(vec[:, V_GF + 2 * q:V_GF + 2 * q + 2], ITEM), ALU.mult).then_inc(xT_evac, 1)

            take_xT(0)
            dve.sem_inc(glu_read, 2)
            dve.sem_inc(act_ready, 2)
            per_item = NF * 2
            start = step.n
            with dve.Fori(0, ITEMS) as i:
                with dve.If(i < last):
                    step.base, step.n = start + per_item * i, 0
                    e = dve.value_load(item_e[0:1, bass.ds(i, 1)], min_val=0, max_val=N_EXP - 1)
                    col = dve.value_load(item_col[0:1, bass.ds(i, 1)], min_val=0, max_val=N_EXP * LISTS - 2)
                    nxt = dve.value_load(item_col[0:1, bass.ds(i + 1, 1)], min_val=0, max_val=N_EXP * LISTS - 2)
                    dve.wait_ge(lin_read, 8 * i + 2)
                    dve.tensor_copy(cur_b[:, :], b_gu[:, bass.ds(e, 1), :]).then_inc(cur_b_ready, 1)
                    dve.wait_ge(xg_in, 32 * i + 32)
                    dve.tensor_copy(cur_x[:, :], x_idx[:, bass.ds(nxt, 2)]).then_inc(cur_x_ready, 1)
                    dve.wait_ge(cur_b_ready, i + 1)
                    dve.wait_ge(yT_ps, 8 * i + 1)
                    for j in range(NF):
                        dve.wait_ge(lin_read, 8 * i + j + 3)
                        dve.tensor_scalar(glu_t[:, j % 2, :], bank(j % 2)[:, 0:256], cur_b[:, j:j + 1], LIMIT,
                                          ALU.add, ALU.min).then_inc(glu_read, 1)
                        step.do(dve.tensor_scalar(lin_c[:, j % 2, :], lin_b[:, j % 2, :], LIMIT, -LIMIT,
                                                  ALU.min, ALU.max))
                        dve.wait_ge(sig_ready, 8 * i + j + 1)
                        step.do(dve.tensor_tensor(glu_s[:, j % 2, :], glu_t[:, j % 2, :], glu_s[:, j % 2, :], ALU.mult))
                        dve.scalar_tensor_tensor(out=actT[:, j, :], in0=lin_c[:, j % 2, :], scalar=1.0,
                                                 in1=glu_s[:, j % 2, :], op0=ALU.add, op1=ALU.mult).then_inc(act_ready, 1)
                    take_xT(i + 1)
                    dve.wait_ge(y_sent, i + 1)
                    dve.tensor_copy(cur_y[:, :], y_idx[:, bass.ds(col, 2)]).then_inc(cur_y_ready, 1)
                    assert step.n == per_item

            dve.wait_ge(y_sent, last + 1)
            dve.wait_ge(gain_in, 16)
            tail = Steps(dve, tail_step)
            for t in range(NT):
                dve.wait_ge(y_back[t % 4], 16 * (t // 4 + 1))
                for c in range(TOP_K):
                    ins = dve.scalar_tensor_tensor(out=x1[:, t, :], in0=y_in[t % 4][:, c, :], scalar=gate[:, t, c:c + 1],
                                                   in1=x1[:, t, :], op0=ALU.mult, op1=ALU.add)
                    if c < TOP_K - 1:
                        tail.do(ins)
                ins.then_inc(y_sum, 1)
                dve.wait_ge(y_sum, t + 1)
                if t >= 3:
                    dve.wait_ge(out_sent[t % 3], 16 * (t // 3))
                tail.do(dve.tensor_tensor_reduce(out_sb[:, t % 3, :], x1[:, t, :], x1[:, t, :], 1.0, 0.0,
                                                 ALU.mult, ALU.add, ssq[:, t:t + 1]))
                dve.tensor_scalar(ssq[:, t:t + 1], ssq[:, t:t + 1], 1.0 / D, EPS, ALU.mult, ALU.add).then_inc(mean_sq, 1)
                dve.wait_ge(rstd_ready, 4 * NT + t + 1)
                dve.scalar_tensor_tensor(out=out_sb[:, t % 3, :], in0=x1[:, t, :], scalar=rstd[:, t:t + 1],
                                         in1=gain_wide, op0=ALU.mult, op1=ALU.mult).then_inc(out_ready, 1)


_INS = ['x', 'norm_attn_g', 'w_in', 'rel_bias_table', 'lambda_q1', 'lambda_k1', 'lambda_q2', 'lambda_k2',
        'diff_norm_g', 'mlstm_conv_w', 'mlstm_conv_b', 'mlstm_gate_b', 'mlstm_o_b', 'mlstm_norm_g', 'w_out',
        'norm_ffn_g', 'router_w', 'router_b', 'expert_w_gu', 'expert_b_gu', 'expert_w_down', 'expert_b_down',
        'final_norm_g']


def kernel(**inputs):
    import concourse.bacc as bacc
    from concourse.bass_utils import run_bass_kernel_spmd as run

    nc = bacc.Bacc("TRN2", target_bir_lowering=False, num_devices=1)
    arrays, args = {}, []
    for name, a in [(n, inputs[n]) for n in _INS] + [("buckets", bucket_rows())]:
        a = np.ascontiguousarray(a)
        arrays[f"in_{name}_dram"] = a
        args.append(nc.dram_tensor(f"in_{name}_dram", a.shape, mybir.dt.from_np(a.dtype), kind="ExternalInput").ap())
    args.append(nc.dram_tensor("out_0_dram", (1, SEQ, D), F32, kind="ExternalOutput").ap())
    build(nc, *args)
    r = run(nc, [arrays], core_ids=[0])
    return r.results[0]["out_0_dram"]
```

```python
import math
from contextlib import ExitStack

import numpy as np
import concourse.bass as bass
from concourse import mybir

F32 = mybir.dt.float32
I32 = mybir.dt.int32
U32 = mybir.dt.uint32
ALU = mybir.AluOpType
ACT = mybir.ActivationFunctionType
AX = mybir.AxisListType.X

P = 128
SEQ = 1024
D = 1024
NT = SEQ // P
KD = D // P
HALF = 512
DAH, DQ, DV = 4, 64, 128
MLH = 4
IN_COLS = 3080
EPS = 1e-5
REL_BUCKETS, REL_MAX_DIST = 32, 128
STRIP = SEQ + P - 1
MASKED = -1e30
N_EXP, TOP_K, D_FF = 32, 4, 1024
NF = D_FF // P
LIMIT, ALPHA = 7.0, 1.702
ITEM = 256
LISTS = SEQ // P
MAX_EXTRA = 15
ITEMS = N_EXP + MAX_EXTRA
ROUNDS = SEQ // ITEM - 1
WIDTHS = list(range(64, ITEM + 1, 8))
NO_ROW = 1 << 20
V_GA, V_GF, V_GD, V_GM, V_CW, V_CB, V_OB, V_ROWS = 0, 8, 16, 20, 24, 40, 44, 48
LAM_INIT = 0.8 - 0.6 * math.exp(-0.3 * 0)


def bucket_rows():
    rel = np.arange(SEQ - 1, -1, -1)
    exact = REL_BUCKETS // 2
    large = exact + (np.log(np.maximum(rel, 1).astype(np.float32) / exact) / math.log(REL_MAX_DIST / exact)
                     * (REL_BUCKETS - exact)).astype(np.int32)
    bucket = np.where(rel < exact, rel, np.minimum(large, REL_BUCKETS - 1))
    return (np.arange(REL_BUCKETS)[:, None] == bucket[None, :]).astype(np.float32)


class Steps:

    def __init__(self, eng, sem):
        self.eng, self.sem, self.n, self.base = eng, sem, 0, 0

    def do(self, ins):
        self.n += 1
        ins.then_inc(self.sem, 1)
        self.eng.wait_ge(self.sem, self.base + self.n)


def build(nc, x, norm_attn_g, w_in, rel_bias_table, lambda_q1, lambda_k1, lambda_q2, lambda_k2,
          diff_norm_g, mlstm_conv_w, mlstm_conv_b, mlstm_gate_b, mlstm_o_b, mlstm_norm_g, w_out,
          norm_ffn_g, router_w, router_b, expert_w_gu, expert_b_gu, expert_w_down, expert_b_down,
          final_norm_g, buckets, out):
    x_rows = x.rearrange("b (t p) d -> (b t) p d", p=P)
    out_rows = out.rearrange("b (t p) d -> (b t) p d", p=P)
    w_in_k = w_in.rearrange("l (k p) n -> p (l k) n", p=P)
    w_out_k = w_out.rearrange("l (k p) n -> p (l k) n", p=P)
    w_gu = expert_w_gu.rearrange("l e (k p) (h f) -> (l e) h p k f", p=P, h=2)
    w_down = expert_w_down.rearrange("l e (k p) n -> (l e) p k n", p=P)
    strip_dram = nc.dram_tensor("strip_dram", [DAH, STRIP + 1], F32).ap()
    h2_dram = nc.dram_tensor("h2_dram", [SEQ, D], F32).ap()
    y_dram = nc.dram_tensor("y_dram", [SEQ * TOP_K, D], F32).ap()
    list_dram = nc.dram_tensor("list_dram", [P * N_EXP * LISTS, 1], I32).ap()

    with ExitStack() as ctx:
        def sb(name, shape, dt=F32):
            return ctx.enter_context(nc.sbuf_tensor(name, shape, dt))

        def sem(name):
            return ctx.enter_context(nc.semaphore(name))

        PS = ctx.enter_context(nc.psum_tensor("PS", [P, 8, HALF], F32))

        def bank(b):
            return PS[:, b, :]

        def banks2(b):
            return PS[:, b:b + 2, :].rearrange("p b n -> p (b n)")

        unit = [sb(f"unit{i}", [P, 4128 if i == 0 else 4096]) for i in range(6)]
        pairA, pairB = sb("pairA", [P, 8192]), sb("pairB", [P, 8192])
        unit10, unit11 = sb("unit10", [P, 4096]), sb("unit11", [P, 4096])
        scratch = sb("scratch", [P, 1024])

        def kn(t, k=KD):
            return t.rearrange("p (k n) -> p k n", k=k)

        group_w = [kn(unit[i][:, 0:4096]) for i in (2, 3, 0, 1, 4, 5)]
        x_raw = kn(pairB[:, :])
        hT = kn(pairA[:, :])
        one_hot = unit11[0:REL_BUCKETS, 0:SEQ]
        strip_row = unit11[0:DAH, SEQ:SEQ + STRIP + 1]
        gate_w = kn(unit11[:, 3600:3888])
        vec_rows = unit11[0:V_ROWS, 3888:4016]
        squares = kn(unit10[:, 0:2048], 2)
        ml_raw = kn(unit10[:, :], 4)
        ml_qk = kn(unit[2][:, :], 4)
        ml_sig = kn(unit[3][:, :], 4)
        da_q = kn(unit11[:, :], DAH)
        da_k = kn(pairB[:, 0:4096], DAH)
        da_v = kn(pairB[:, 4096:8192])
        gate_rows = pairB[:, 4096:5120]
        row_a, row_b, row_c = (pairB[0:MLH, 5120 + 1024 * i:6144 + 1024 * i] for i in range(3))
        row_g = pairB[0:MLH, 4096:5120]
        ml_v = unit[0][:, 0:NT * MLH * (DV + 1)].rearrange("p (t h d) -> p t h d", t=NT, h=MLH)
        o_gate = kn(unit[1][:, :], 4)
        m_wide = kn(unit[3][:, :], MLH)
        ml_decay = [unit10[:, 0:512], unit10[:, 512:1024], scratch[:, 0:512]]
        ml_w = [unit10[:, 1024:1536], unit10[:, 1536:2048], scratch[:, 512:1024]]
        ml_e = kn(unit10[:, 2048:2304], 2)
        ml_h = unit10[:, 2304:2820].rearrange("p (h d) -> p h d", h=MLH)
        ml_hr = kn(unit10[:, 2820:3332], MLH)
        ml_sq = kn(unit10[:, 3332:3844], MLH)
        above = unit10[:, 3844:3972]
        pick = kn(scratch[:, 0:512], 4)
        lam_in = kn(scratch[:, 512:768], 4)
        flip = scratch[:, 768:768 + P]
        strip = kn(unit[4][:, :], DAH)
        prob = [[u[:, 0:1024], u[:, 1024:2048]] for u in (unit[3], unit10)]
        prob.append([u[:, 3072:4096] for u in (unit[3], unit10)])
        probT = kn(unit[3][:, 2048:3072], 2)
        da_o = kn(unit10[:, 2048:2560], DAH)
        da_sq = kn(unit10[:, 2560:3072], DAH)
        mixT = kn(pairA[:, :])
        w_o = [kn(unit[5][:, :], 4), kn(unit[2][:, :], 4)]
        x1 = kn(pairB[:, :])
        h2 = kn(unit10[:, 0:2048], 2)
        h2T = [kn(unit10[:, 2048 + 1024 * i:3072 + 1024 * i]) for i in range(2)]
        x_again = kn(unit11[:, 0:2048], 2)
        b_gu_rows = unit11[0:N_EXP, 2048:4096]
        chosen = scratch[:, :].rearrange("p (t c e) -> p t c e", t=NT, c=TOP_K)
        b_down = pairA[:, 6144:7168]
        g_allT = kn(pairA[:, 7168:8192])
        n_flags = ROUNDS * N_EXP
        flag, pos, pos2, val_c, packed = (unit10[0:1, n_flags * i:n_flags * (i + 1)] for i in range(5))
        eq = kn(unit10[0:1, 1024:1024 + MAX_EXTRA * n_flags], MAX_EXTRA)
        order = kn(unit11[0:1, 2048:2048 + MAX_EXTRA * n_flags], MAX_EXTRA)
        got = unit11[0:1, 3584:3584 + MAX_EXTRA]
        xg = kn(pairA[:, 0:2048], 2)
        xT = kn(pairA[:, 2048:4096])
        actT = kn(pairA[:, 4096:6144])
        y_rows = kn(pairA[:, 6144:8192], 2)
        gu_w = [unit[i][:, 0:4096].rearrange("p (h k f) -> p h k f", h=2, k=KD) for i in range(4)]
        down_w = [kn(unit[4 + c // 2][:, 2048 * (c % 2):2048 * (c % 2) + 2048]) for c in range(4)]
        yT = kn(unit10[:, 2048:4096])
        glu_t = kn(unit10[:, 0:512], 2)
        glu_s = kn(unit10[:, 512:1024], 2)
        lin_b = kn(unit10[:, 1024:1536], 2)
        lin_c = kn(unit10[:, 1536:2048], 2)
        y_in = [unit[i][:, 0:4096].rearrange("p (c d) -> p c d", c=TOP_K) for i in range(4)]
        gain_wide = unit11[:, 0:1024]
        sum_squares = kn(unit10[:, 0:2048], 2)
        out_sb = kn(unit11[:, 1024:4096], 3)

        ident, ones, before = sb("ident", [P, P]), sb("ones", [P, P]), sb("before", [P, P])
        vec = sb("vec", [P, V_ROWS])
        gd_scaled = sb("gd_scaled", [P, DAH])
        gate_bias = sb("gate_bias", [64, 1])
        neg_half = sb("neg_half", [P, NT])
        ssq, rstd = sb("ssq", [P, NT]), sb("rstd", [P, NT])
        table = sb("table", [REL_BUCKETS, DAH])
        lam = sb("lam", [P, 4])
        a_col, em_col = sb("a_col", [P, NT, MLH]), sb("em_col", [P, NT, MLH])
        small = sb("small", [P, 32])
        rw = sb("rw", [P, KD, N_EXP])
        rb_wide = sb("rb_wide", [P, N_EXP])
        lanes = sb("lanes", [P, N_EXP])
        lg, top8 = sb("lg", [P, N_EXP]), sb("top8", [P, 8])
        idx8 = sb("idx8", [P, 8], U32)
        idxf = sb("idxf", [P, NT, TOP_K])
        gate = sb("gate", [P, NT, TOP_K])
        mask = sb("mask", [P, NT, N_EXP])
        g_all = sb("g_all", [P, NT, N_EXP])
        slot = sb("slot", [P, NT, TOP_K])
        slot_i, slot_lo, slot_hi = (sb(n, [P, NT, TOP_K], I32) for n in ("slot_i", "slot_lo", "slot_hi"))
        where = sb("where", [P, NT, TOP_K], I32)
        row_id = sb("row_id", [P, NT, TOP_K], I32)
        y_idx, x_idx = sb("y_idx", [P, N_EXP * LISTS], I32), sb("x_idx", [P, N_EXP * LISTS], I32)
        cur_x, cur_y = sb("cur_x", [P, 2], I32), sb("cur_y", [P, 2], I32)
        b_gu = sb("b_gu", [P, N_EXP, 2 * NF])
        cur_b = sb("cur_b", [P, 2 * NF])
        counts = sb("counts", [P, N_EXP])
        item_e, item_col, item_n = (sb(n, [1, ITEMS + 1], I32) for n in ("item_e", "item_col", "item_n"))
        n_items, got_i = sb("n_items", [1, 1], I32), sb("got_i", [1, MAX_EXTRA], I32)

        x_in = [sem(f"x_in{t}") for t in range(NT)]
        group_in = [sem(f"group_in{g}") for g in range(6)]
        (small_in, consts, vec_ps, vec_ready, strip_ps, strip_row_ready, strip_out, strip_in, mean_sq,
         rstd_ready, x_scaled, x_turned, hT_ready, proj_done, proj_evac, conv_done, sig_done, qk_done,
         log_f_part, em_in, em_ready, cols_ps, cols_ready, wide_ps, wide_ready,
         dve_step, act_step, pool_step) = (sem(n) for n in (
             "small_in", "consts", "vec_ps", "vec_ready", "strip_ps", "strip_row_ready", "strip_out",
             "strip_in", "mean_sq", "rstd_ready", "x_scaled", "x_turned", "hT_ready", "proj_done",
             "proj_evac", "conv_done", "sig_done", "qk_done", "log_f_part", "em_in", "em_ready",
             "cols_ps", "cols_ready", "wide_ps", "wide_ready", "dve_step", "act_step",
             "pool_step"))
        (ml_s_done, ml_e_ready, ml_d_ready, ml_w_ready, ml_h_done, ml_h_read, ml_norm_ready, ml_turned,
         ml_mixed, da_logits, da_max, da_exp, da_a_ready, da_aT_ps, da_aT_ready, da_o_done, da_o_read,
         da_norm_ready, da_turned, da_mixed, w_out_in0, w_out_in1) = (sem(n) for n in (
             "ml_s_done", "ml_e_ready", "ml_d_ready", "ml_w_ready", "ml_h_done", "ml_h_read",
             "ml_norm_ready", "ml_turned", "ml_mixed", "da_logits", "da_max", "da_exp", "da_a_ready",
             "da_aT_ps", "da_aT_ready", "da_o_done", "da_o_read", "da_norm_ready", "da_turned", "da_mixed",
             "w_out_in0", "w_out_in1"))
        x_again_in = [sem(f"x_again_in{i}") for i in range(2)]
        h2_out = [sem(f"h2_out{i}") for i in range(2)]
        (out_proj_done, x1_ready, h2_ready, h2_turned, h2T_ready, logits_done, top_ready, gate_exp,
         chosen_ready, pos_ps, place_read, where_ready, list_clear, list_out, list_in, g_turned,
         g_allT_ready, down_bias_done, x1_full, b_gu_turned, b_gu_ready, b_down_in, items_ready,
         x_idx_ready, row_ids) = (sem(n) for n in (
             "out_proj_done", "x1_ready", "h2_ready", "h2_turned", "h2T_ready", "logits_done", "top_ready",
             "gate_exp", "chosen_ready", "pos_ps", "place_read", "where_ready", "list_clear", "list_out",
             "list_in", "g_turned", "g_allT_ready", "down_bias_done", "x1_full", "b_gu_turned",
             "b_gu_ready", "b_down_in", "items_ready", "x_idx_ready", "row_ids"))
        gu_in = [sem(f"gu_in{c}") for c in range(4)]
        down_in = [sem(f"down_in{c}") for c in range(4)]
        (cur_x_ready, cur_y_ready, cur_b_ready, xg_in, xT_ps, xT_evac, gu_done, glu_read, lin_read,
         sig_ready, act_ready, yT_ps, yT_evac, y_ps, y_evac, y_out, gain_in, y_sum, out_ready) = (
            sem(n) for n in (
                "cur_x_ready", "cur_y_ready", "cur_b_ready", "xg_in", "xT_ps", "xT_evac", "gu_done",
                "glu_read", "lin_read", "sig_ready", "act_ready", "yT_ps", "yT_evac", "y_ps", "y_evac", "y_out",
                "gain_in", "y_sum", "out_ready"))
        lam_ready, lam_exp, item_iotas, tail_step, b_gu_in, v_ones = (sem(n) for n in (
            "lam_ready", "lam_exp", "item_iotas", "tail_step", "b_gu_in", "v_ones"))
        gate_bias_clear, pool_waited, y_sent, strip_flipped, strip_ready = (sem(n) for n in (
            "gate_bias_clear", "pool_waited", "y_sent", "strip_flipped", "strip_ready"))
        ident_ready, table_in, gate_w_in, lam_in_sem, router_in, squared, gain_rows_in, bias_clear, ml_divided, \
            ml_squared, da_squared, sum_squared = (sem(n) for n in (
            "ident_ready", "table_in", "gate_w_in", "lambda_in", "router_in", "squared",
            "gain_rows_in", "bias_clear", "ml_divided", "ml_squared", "da_squared",
            "sum_squared"))
        y_back = [sem(f"y_back{i}") for i in range(4)]
        out_sent = [sem(f"out_sent{i}") for i in range(3)]

        def wide(ap, n):
            return ap.unsqueeze(len(ap.shape)).broadcast_to(list(ap.shape) + [n])

        def again(ap, n):
            return ap.unsqueeze(1).broadcast_to([ap.shape[0], n, ap.shape[1]])

        QKM, Q, K, V, MV, MO, GATE = range(7)
        outs = [(QKM, h, m) for h in range(2) for m in range(4)] + [(GATE, 0, 0), (GATE, 1, 0)]
        for g in (Q, K):
            outs += [(g, h, m) for h in range(2) for m in range(4)]
        outs += [(V, 0, t) for t in range(NT)] + [(MV, 0, t) for t in range(NT)]
        outs += [(MO, h, m) for h in range(2) for m in range(4)]
        N_OUTS = len(outs)
        after_group = {g: 1 + max(o for o, (k, _, _) in enumerate(outs) if k == g) for g in range(7)}

        ml_units = [(t, h, list(range(j, min(j + 4, t + 1)))) for t in range(NT) for h in range(MLH)
                    for j in range(0, t + 1, 4)]
        ml_tile_end = [max(u for u, (t, _, _) in enumerate(ml_units) if t == n) + 1 for n in range(NT)]
        ml_bank = (0, 1, 6)
        ml_diagonal = [u for u, (t, _, js) in enumerate(ml_units) if js[-1] == t]
        da_units = [(t, h) for t in range(NT) for h in range(DAH)]
        da_groups = []
        for t, h in da_units:
            da_groups.append([list(range(j, min(j + 4, t + 1))) for j in range(0, t + 1, 4)])
        N_SMALL = 6 + 2

        block = ctx.enter_context(nc.Block())

        @block.sync
        def _(sp):
            first_col = [1536, 0, 512, 1024, 2048, 2560]

            def load_group(g):
                c = first_col[g]
                sp.dma_start(group_w[g], w_in_k[:, :, c:c + HALF]).then_inc(group_in[g], 16)

            for t in range(4):
                sp.dma_start(x_raw[:, t, :], x_rows[t]).then_inc(x_in[t], 16)
            load_group(QKM)
            for t in range(4, NT):
                sp.dma_start(x_raw[:, t, :], x_rows[t]).then_inc(x_in[t], 16)
            sp.wait_ge(consts, 1)
            for lo, c in ((0, 3072), (32, 3076)):
                sp.dma_start(gate_w[:, :, lo:lo + 4], w_in_k[:, :, c:c + 4]).then_inc(gate_w_in, 16)
            for g in range(Q, MO + 1):
                load_group(g)
            for n, v in enumerate((lambda_q1, lambda_k1, lambda_q2, lambda_k2)):
                sp.dma_start(lam_in[:, n, :], v.rearrange("l d -> (l d)").partition_broadcast(P)).then_inc(lam_in_sem, 16)
            sp.dma_start(rb_wide[:, :], router_b.rearrange("l d -> (l d)").partition_broadcast(P)).then_inc(router_in, 16)
            sp.dma_start(rw[:, :, :], router_w.rearrange("l (k p) e -> p (l k) e", p=P)).then_inc(router_in, 16)
            sp.wait_ge(strip_row_ready, 3)
            sp.dma_start(strip_dram, strip_row).then_inc(strip_out, 16)
            sp.wait_ge(strip_out, 16)
            sp.wait_ge(proj_done, after_group[MV])
            shifted = bass.AP(strip_dram.tensor, 0, [[1, P], [STRIP + 1, DAH], [1, SEQ]])
            sp.dma_start(strip, shifted).then_inc(strip_in, 16)
            sp.wait_ge(proj_done, after_group[MO])
            sp.dma_start(w_o[0], w_out_k[:, 0:4, :]).then_inc(w_out_in0, 16)
            sp.wait_ge(ml_h_done, len(ml_units))
            sp.dma_start(w_o[1], w_out_k[:, 4:8, :]).then_inc(w_out_in1, 16)

            def load_gu(c, e):
                for h in range(2):
                    sp.dma_start(gu_w[c][:, h], w_gu[e, h, :, :, 256 * c:256 * c + 256]).then_inc(gu_in[c], 16)

            def load_down(c, e):
                sp.dma_start(down_w[c], w_down[e, :, :, 256 * c:256 * c + 256]).then_inc(down_in[c], 16)

            load_gu(0, 0)
            sp.wait_ge(ml_mixed, NT)
            load_gu(1, 0)
            sp.wait_ge(da_mixed, NT)
            load_gu(3, 0)
            load_down(0, 0)
            load_down(1, 0)
            for t in range(2):
                sp.dma_start(x_again[:, t, :], x_rows[t]).then_inc(x_again_in[t], 16)
            sp.dma_start(b_gu_rows, expert_b_gu.rearrange("l e f -> (l e) f")).then_inc(b_gu_in, 16)
            for t in range(NT):
                sp.wait_ge(h2_ready, t + 1)
                sp.dma_start(h2_dram[P * t:P * t + P, :], h2[:, t % 2, :]).then_inc(h2_out[t % 2], 16)
                if t + 2 < NT:
                    sp.dma_start(x_again[:, t % 2, :], x_rows[t + 2]).then_inc(x_again_in[t % 2], 16)
            sp.wait_ge(out_proj_done, NT)
            load_gu(2, 0)
            load_down(2, 0)
            load_down(3, 0)
            sp.wait_ge(bias_clear, 1)
            sp.dma_start(b_down[0:N_EXP, :], expert_b_down.rearrange("l e d -> (l e) d")).then_inc(b_down_in, 16)
            sp.wait_ge(list_out, 16 * NT * TOP_K)
            sp.dma_start(y_idx[:, :], list_dram.rearrange("(p c) o -> p (c o)", p=P)).then_inc(list_in, 16)

            def item_weights(i, e):
                for c in range(4):
                    sp.wait_ge(gu_done, 8 * (i - 1) + 2 * c + 2)
                    load_gu(c, e)
                for c in range(4):
                    sp.wait_ge(yT_ps, 8 * (i - 1) + 2 * c + 3)
                    load_down(c, e)

            with sp.Fori(1, N_EXP) as i:
                item_weights(i, i)
            sp.wait_ge(items_ready, 1)
            last = sp.value_load(n_items[0:1, 0:1], min_val=N_EXP, max_val=ITEMS)
            with sp.Fori(N_EXP, ITEMS) as i:
                with sp.If(i < last):
                    item_weights(i, sp.value_load(item_e[0:1, bass.ds(i, 1)], min_val=0, max_val=N_EXP - 1))
            sp.wait_ge(y_sent, last + 1)
            sp.dma_start(gain_wide, final_norm_g.partition_broadcast(P)).then_inc(gain_in, 16)
            for t in range(NT):
                if t >= 4:
                    sp.wait_ge(y_sum, t - 3)
                sp.dma_start(y_in[t % 4], y_dram[P * TOP_K * t:P * TOP_K * (t + 1), :]
                             .rearrange("(p c) d -> p c d", c=TOP_K)).then_inc(y_back[t % 4], 16)
            for i in range(3):
                sp.wait_ge(out_sent[i], 16 * len(range(i, NT, 3)))

        @block.gpsimd
        def _(pool):
            step = Steps(pool, pool_step)
            pool.memset(gate_bias[:, :], 0.0).then_inc(gate_bias_clear, 1)
            step.do(pool.memset(ident[:, :], 0.0))
            pool.affine_select(out=ident[:, :], in_=ident[:, :], compare_op=ALU.not_equal, fill=1.0, base=0,
                               pattern=[[-1, P]], channel_multiplier=1).then_inc(ident_ready, 1)
            pool.memset(gate_w, 0.0).then_inc(consts, 1)
            pool.memset(neg_half[:, :], -0.5).then_inc(consts, 1)
            pool.memset(ones[:, :], 1.0).then_inc(consts, 1)
            step.do(pool.memset(pick, 0.0))
            pool.affine_select(out=pick, in_=pick, compare_op=ALU.not_equal, fill=1.0, base=0,
                               pattern=[[-1, 4], [0, P]], channel_multiplier=1).then_inc(consts, 1)
            step.do(pool.memset(flip, 0.0))
            pool.affine_select(out=flip, in_=flip, compare_op=ALU.not_equal, fill=1.0, base=1 - P,
                               pattern=[[1, P]], channel_multiplier=1).then_inc(consts, 1)
            pool.memset(strip_row[:, SEQ:STRIP + 1], MASKED).then_inc(strip_row_ready, 1)
            step.do(pool.memset(before[:, :], 1.0))
            pool.affine_select(out=before[:, :], in_=before[:, :], compare_op=ALU.is_gt, fill=0.0, base=0,
                               pattern=[[1, P]], channel_multiplier=-1).then_inc(consts, 1)
            for t in range(NT):
                pool.wait_ge(mean_sq, t + 1)
                pool.tensor_tensor(rstd[:, t:t + 1], ssq[:, t:t + 1], neg_half[:, 0:1],
                                   ALU.pow).then_inc(rstd_ready, 1)
            pool.iota(lanes[:, :], pattern=[[1, N_EXP]], base=0, channel_multiplier=0,
                      allow_small_or_imprecise_dtypes=True).then_inc(row_ids, 1)
            pool.iota(row_id[:, :, :], pattern=[[P * TOP_K, NT], [1, TOP_K]], base=0,
                      channel_multiplier=TOP_K).then_inc(row_ids, 1)
            step.do(pool.memset(y_idx[:, :], NO_ROW))
            pool.dma_start(list_dram.rearrange("(p c) o -> p (c o)", p=P), y_idx[:, :]).then_inc(list_clear, 16)
            pool.wait_ge(qk_done, 4)
            step.do(pool.memset(above, 0.0))
            pool.affine_select(out=above, in_=above, compare_op=ALU.is_ge, fill=1e4, base=0,
                               pattern=[[1, P]], channel_multiplier=-1).then_inc(consts, 1)
            for n in range(NT):
                pool.wait_ge(mean_sq, NT + n + 1)
                pool.tensor_tensor(small[:, 4:8], small[:, 0:4], neg_half[:, 0:4], ALU.pow).then_inc(rstd_ready, 1)
            for n in range(NT):
                pool.wait_ge(mean_sq, 2 * NT + n + 1)
                pool.tensor_tensor(small[:, 4:8], small[:, 0:4], neg_half[:, 0:4], ALU.pow).then_inc(rstd_ready, 1)
            def x1_rstd(t):
                pool.wait_ge(mean_sq, 3 * NT + t + 1)
                pool.tensor_tensor(rstd[:, t:t + 1], ssq[:, t:t + 1], neg_half[:, 0:1],
                                   ALU.pow).then_inc(rstd_ready, 1)

            def to_lists(t):
                pool.wait_ge(where_ready, t + 1)
                pool.sem_inc(pool_waited, 1)
                for c in range(TOP_K):
                    pool.indirect_dma_start(
                        out=list_dram, out_offset=bass.IndirectOffsetOnAxis(ap=where[:, t, c:c + 1], axis=0),
                        in_=row_id[:, t, c:c + 1], in_offset=None).then_inc(list_out, 16)

            pool.wait_ge(list_clear, 16)
            x1_rstd(0)
            x1_rstd(1)
            for t in range(2, NT):
                x1_rstd(t)
                to_lists(t - 2)
            to_lists(NT - 2)
            for i in range(2):
                pool.wait_ge(h2_out[i], 16 * NT // 2)
            pool.wait_ge(logits_done, NT)
            pool.wait_ge(b_gu_turned, 1)
            pool.iota(val_c, pattern=[[2, ROUNDS], [LISTS, N_EXP]], base=2, channel_multiplier=0,
                      allow_small_or_imprecise_dtypes=True).then_inc(item_iotas, 1)
            pool.iota(order, pattern=[[1, MAX_EXTRA], [0, ROUNDS * N_EXP]], base=1, channel_multiplier=0,
                      allow_small_or_imprecise_dtypes=True).then_inc(item_iotas, 1)
            to_lists(NT - 1)

            last_x, last_y = pool.to_reg(SEQ - 1), pool.to_reg(SEQ * TOP_K - 1)

            def gather(i):
                for b in range(2):
                    pool.indirect_dma_start(
                        out=xg[:, b, :], out_offset=None, in_=h2_dram,
                        in_offset=bass.IndirectOffsetOnAxis(ap=cur_x[:, b:b + 1], axis=0),
                        bounds_check=last_x, oob_is_err=False).then_inc(xg_in, 16)

            pool.wait_ge(out_proj_done, NT)
            pool.wait_ge(cur_x_ready, 1)
            pool.sem_inc(pool_waited, 1)
            gather(0)
            pool.wait_ge(items_ready, 1)
            last = pool.value_load(n_items[0:1, 0:1], min_val=N_EXP, max_val=ITEMS)
            with pool.Fori(0, ITEMS) as i:
                with pool.If(i < last):
                    pool.wait_ge(cur_x_ready, i + 2)
                    pool.wait_ge(xT_ps, 4 * i + 4)
                    pool.sem_inc(pool_waited, 1)
                    gather(i + 1)
                    pool.wait_ge(cur_y_ready, i + 1)
                    pool.wait_ge(y_evac, 4 * i + 5)
                    pool.sem_inc(pool_waited, 1)
                    for b in range(2):
                        pool.indirect_dma_start(
                            out=y_dram, out_offset=bass.IndirectOffsetOnAxis(ap=cur_y[:, b:b + 1], axis=0),
                            in_=y_rows[:, b, :], in_offset=None,
                            bounds_check=last_y, oob_is_err=False).then_inc(y_out, 16)
                    pool.wait_ge(y_out, 32 * i + 32)
                    pool.sem_inc(y_sent, 1)
            for t in range(NT):
                pool.wait_ge(mean_sq, 4 * NT + t + 1)
                pool.tensor_tensor(rstd[:, t:t + 1], ssq[:, t:t + 1], neg_half[:, 0:1],
                                   ALU.pow).then_inc(rstd_ready, 1)
            pool.wait_ge(xg_in, 32 * last + 32)

        @block.tensor
        def _(pe):
            pe.wait_ge(ident_ready, 1)
            def turn_x(t):
                pe.wait_ge(x_scaled, t + 1)
                if t >= 2:
                    pe.wait_ge(hT_ready, t - 1)
                for k in range(KD):
                    ins = pe.transpose(bank(4 + 2 * (t % 2) + k // 4)[:, P * (k % 4):P * (k % 4) + P],
                                       x_raw[:, t, P * k:P * k + P], ident[:, :])
                ins.then_inc(x_turned, 1)

            def project(o):
                kind, a, b = outs[o]
                if kind < 6:
                    pe.wait_ge(group_in[kind], 16)
                if kind in (QKM, Q, K, MO, GATE):
                    pe.wait_ge(hT_ready, 4 * a + 4)
                if o >= 4:
                    pe.wait_ge(proj_evac, o - 3)
                elif o == 0:
                    pe.wait_ge(vec_ready, 1)
                if kind == GATE:
                    pe.wait_ge(gate_w_in, 32)
                for k in range(KD):
                    if kind in (V, MV):
                        ps, lhs, rhs = bank(o % 4), hT[:, k, P * b:P * b + P], group_w[kind][:, k, :]
                    elif kind == GATE:
                        ps, lhs, rhs = bank(o % 4)[0:36, :], gate_w[:, k, :], hT[:, k, HALF * a:HALF * a + HALF]
                    else:
                        ps, lhs = bank(o % 4), group_w[kind][:, k, P * b:P * b + P]
                        rhs = hT[:, k, HALF * a:HALF * a + HALF]
                    ins = pe.matmul(ps, lhs, rhs, start=(k == 0), stop=(k == KD - 1))
                ins.then_inc(proj_done, 1)

            turn_x(0)
            pe.wait_ge(gain_rows_in, 16)
            pe.transpose(bank(0)[:, 0:KD], vec_rows[V_GA:V_GA + KD, :], ident[0:KD, 0:KD]).then_inc(vec_ps, 1)
            for t in range(1, 4):
                turn_x(t)
            for o in range(4):
                project(o)
            for t in range(4, NT):
                turn_x(t)
            pe.wait_ge(hT_ready, NT)
            pe.wait_ge(small_in, 16 * N_SMALL)
            pe.transpose(bank(5)[:, 0:V_ROWS], vec_rows, ident[0:V_ROWS, 0:V_ROWS]).then_inc(vec_ps, 1)
            pe.wait_ge(table_in, 32)
            for half in range(2):
                pe.matmul(bank(6 + half)[0:DAH, :], table[:, :], one_hot[:, HALF * half:HALF * half + HALF],
                          start=True, stop=True).then_inc(strip_ps, 1)
            for o in range(4, after_group[K]):
                project(o)
            pe.wait_ge(em_ready, 1)
            pe.wait_ge(consts, 6)
            for n, row in enumerate((row_c, row_b)):
                for t in range(NT):
                    ins = pe.transpose(bank(4)[:, 32 * n + 4 * t:32 * n + 4 * t + 4], row[:, P * t:P * t + P],
                                       ident[0:MLH, 0:MLH])
            ins.then_inc(cols_ps, 1)
            for h in range(MLH):
                for half in range(2):
                    n = 2 * h + half
                    if n >= 2:
                        pe.wait_ge(wide_ready, n - 1)
                    pe.matmul(bank(6 + n % 2), pick[0:MLH, h, :], row_a[:, HALF * half:HALF * half + HALF],
                              start=True, stop=True).then_inc(wide_ps, 1)
            for o in range(after_group[K], N_OUTS):
                project(o)

            pe.wait_ge(strip_in, 16)
            for n in range(8):
                if n >= 2:
                    pe.wait_ge(strip_ready, n - 1)
                pe.matmul(bank(6 + n % 2), flip, strip[:, n // 2, HALF * (n % 2):HALF * (n % 2) + HALF],
                          start=True, stop=True).then_inc(strip_flipped, 1)

            def ml_scores(u):
                t, h, js = ml_units[u]
                if u == 2:
                    pe.wait_ge(strip_ready, 8)
                if u >= 3:
                    pe.wait_ge(ml_w_ready, u - 2)
                lo = 64 * (h % 2)
                for n, j in enumerate(js):
                    ins = pe.matmul(bank(ml_bank[u % 3])[:, P * n:P * n + P], ml_qk[lo:lo + 64, 2 + h // 2, P * j:P * j + P],
                                    ml_qk[lo:lo + 64, h // 2, P * t:P * t + P], start=True, stop=True)
                ins.then_inc(ml_s_done, 1)

            def ml_sums(u):
                t, h, js = ml_units[u]
                pe.wait_ge(ml_w_ready, u + 1)
                if h == 0 and js[0] == 0 and t >= 2:
                    pe.wait_ge(ml_h_read, t - 1)
                for n, j in enumerate(js):
                    c = (DV + 1) * (h % 2)
                    ins = pe.matmul(bank(2 + 2 * (t % 2) + h // 2)[:, c:c + DV + 1], ml_w[u % 3][:, P * n:P * n + P],
                                    ml_v[:, j, h, :], start=(j == 0), stop=(j == t))
                ins.then_inc(ml_h_done, 1)

            def ml_turn(t):
                pe.wait_ge(ml_norm_ready, t + 1)
                pe.wait_ge(ml_mixed, t) if t else None
                for h in range(MLH):
                    ins = pe.transpose(bank(7)[:, P * h:P * h + P], ml_hr[:, h, :], ident[:, :])
                ins.then_inc(ml_turned, 1)

            pe.wait_ge(qk_done, 4)
            pe.wait_ge(proj_evac, N_OUTS)
            pe.wait_ge(v_ones, 1)
            ml_scores(0)
            ml_scores(1)
            for u in range(len(ml_units)):
                if u + 2 < len(ml_units):
                    ml_scores(u + 2)
                ml_sums(u)
                for t in range(NT - 1):
                    if u == ml_tile_end[t] + 3:
                        ml_turn(t)

            def da_logit(u):
                t, h = da_units[u]
                if u == 0:
                    pe.wait_ge(ml_h_read, NT)
                for m in range(2):
                    if u:
                        pe.wait_ge(da_max, 2 * u - 1 + m)
                    for c in range(0, t + 1, 4):
                        w = P * min(4, t + 1 - c)
                        ins = pe.matmul(bank(2 * m + c // 4)[:, 0:w], da_q[64 * m:64 * m + 64, h, P * t:P * t + P],
                                        da_k[64 * m:64 * m + 64, h, P * c:P * c + w], start=True, stop=True)
                    ins.then_inc(da_logits, 1)

            da_first = [sum(len(x) for x in da_groups[:u]) for u in range(len(da_units))]

            def da_turn_weights(u):
                pe.wait_ge(da_a_ready, u + 1)
                for n, js in enumerate(da_groups[u]):
                    g = da_first[u] + n
                    if g >= 2:
                        pe.wait_ge(da_aT_ready, g - 1)
                    for i, j in enumerate(js):
                        ins = pe.transpose(bank(4 + g % 2)[:, P * i:P * i + P], prob[u % 3][0][:, P * j:P * j + P],
                                           ident[:, :])
                    ins.then_inc(da_aT_ps, 1)

            def da_values(u):
                t, h = da_units[u]
                if h == 0 and t >= 1:
                    pe.wait_ge(da_o_read, t)
                for n, js in enumerate(da_groups[u]):
                    g = da_first[u] + n
                    pe.wait_ge(da_aT_ready, g + 1)
                    for i, j in enumerate(js):
                        ins = pe.matmul(bank(6)[:, P * h:P * h + P], probT[:, g % 2, P * i:P * i + P],
                                        da_v[:, j, P * h:P * h + P], start=(j == 0), stop=(j == t))
                ins.then_inc(da_o_done, 1)

            def da_turn(t):
                pe.wait_ge(da_norm_ready, t + 1)
                pe.wait_ge(ml_mixed, NT)
                if t:
                    pe.wait_ge(da_mixed, t)
                for h in range(DAH):
                    ins = pe.transpose(bank(7)[:, P * h:P * h + P], da_o[:, h, :], ident[:, :])
                ins.then_inc(da_turned, 1)

            da_logit(0)
            da_logit(1)
            for u in range(2, len(da_units) + 2):
                da_turn_weights(u - 2)
                if u == 2:
                    ml_turn(NT - 1)
                if u < len(da_units):
                    da_logit(u)
                da_values(u - 2)
                if u % DAH == 0 and u > DAH:
                    da_turn(u // DAH - 2)

            def out_project(t):
                if t == 0:
                    pe.wait_ge(w_out_in0, 16)
                    pe.wait_ge(w_out_in1, 16)
                    pe.wait_ge(da_max, 2 * len(da_units))
                pe.wait_ge(da_mixed, t + 1)
                if t >= 2:
                    pe.wait_ge(x1_ready, t - 1)
                for half in range(2):
                    for k in range(KD):
                        ins = pe.matmul(bank(2 * (t % 2) + half), mixT[:, k, P * t:P * t + P],
                                        w_o[k // 4][:, k % 4, HALF * half:HALF * half + HALF],
                                        start=(k == 0), stop=(k == KD - 1))
                ins.then_inc(out_proj_done, 1)

            def turn_h2(t):
                pe.wait_ge(h2_ready, t + 1)
                if t:
                    pe.wait_ge(h2T_ready, 2 * t)
                for k in range(KD):
                    ins = pe.transpose(bank(4 + k // 4)[:, P * (k % 4):P * (k % 4) + P],
                                       h2[:, t % 2, P * k:P * k + P], ident[:, :])
                    if k % 4 == 3:
                        ins.then_inc(h2_turned, 1)

            def route(t):
                pe.wait_ge(h2T_ready, 2 * t + 2)
                if t == 0:
                    pe.wait_ge(router_in, 32)
                if t:
                    pe.wait_ge(top_ready, t)
                for k in range(KD):
                    ins = pe.matmul(bank(6)[:, 0:N_EXP], h2T[t % 2][:, k, :], rw[:, k, :],
                                    start=(k == 0), stop=(k == KD - 1))
                ins.then_inc(logits_done, 1)

            def place(t):
                pe.wait_ge(chosen_ready, t + 1)
                if t:
                    pe.wait_ge(place_read, t)
                for s in range(t + 1):
                    ins = pe.matmul(bank(7)[:, 0:N_EXP], (before if s == t else ones)[:, :], mask[:, s, :],
                                    start=(s == 0), stop=(s == t))
                if t == NT - 1:
                    for s in range(NT):
                        ins = pe.matmul(bank(7)[:, N_EXP:2 * N_EXP], ones[:, :], mask[:, s, :],
                                        start=(s == 0), stop=(s == NT - 1))
                ins.then_inc(pos_ps, 1)

            out_project(0)
            da_turn(NT - 1)
            out_project(1)
            for t in range(NT):
                turn_h2(t)
                if t + 2 < NT:
                    out_project(t + 2)
                if t == NT - 2:
                    pe.wait_ge(b_gu_in, 16)
                    pe.wait_ge(x1_ready, NT - 1)
                    for f in range(2 * NF):
                        ins = pe.transpose(bank(0)[:, 32 * f:32 * f + 32], b_gu_rows[:, P * f:P * f + P],
                                           ident[0:N_EXP, 0:N_EXP])
                    ins.then_inc(b_gu_turned, 1)
                route(t)
                if t:
                    place(t - 1)
            place(NT - 1)
            for t in range(NT):
                ins = pe.transpose(bank(4 + t // 4)[0:N_EXP, P * (t % 4):P * (t % 4) + P], g_all[:, t, :],
                                   ident[:, :])
            ins.then_inc(g_turned, 1)
            pe.wait_ge(g_allT_ready, 2)
            pe.wait_ge(b_down_in, 16)
            pe.wait_ge(x1_ready, NT)
            pe.wait_ge(b_gu_ready, 1)
            for t in range(NT):
                if t >= 2:
                    pe.wait_ge(x1_full, t - 1)
                for half in range(2):
                    ins = pe.matmul(bank(2 * (t % 2) + half), g_allT[:, t, :],
                                    b_down[:, HALF * half:HALF * half + HALF], start=True, stop=True)
                ins.then_inc(down_bias_done, 1)

            def turn_rows(i):
                pe.wait_ge(xg_in, 32 * i + 32)
                for q in range(4):
                    for k in range(2):
                        for b in range(2):
                            ins = pe.transpose(bank(2 + q)[:, 256 * k + P * b:256 * k + P * b + P],
                                               xg[:, b, P * (2 * q + k):P * (2 * q + k) + P], ident[:, :])
                    ins.then_inc(xT_ps, 1)

            def by_width(n, widths, body):
                if len(widths) == 1:
                    body(widths[0])
                    return
                mid = len(widths) // 2
                with pe.If(n <= widths[mid - 1]):
                    by_width(n, widths[:mid], body)
                with pe.Else():
                    by_width(n, widths[mid:], body)

            pe.wait_ge(x1_full, NT)
            turn_rows(0)
            pe.sem_inc(yT_ps, 1)
            pe.sem_inc(y_ps, 1)
            pe.wait_ge(items_ready, 1)
            last = pe.value_load(n_items[0:1, 0:1], min_val=N_EXP, max_val=ITEMS)
            n_next = pe.alloc_register("n_next")
            pe.load(n_next, item_n[0:1, 0:1])
            with pe.Fori(0, ITEMS) as i:
                with pe.If(i < last):
                    n = pe.snap(n_next, min_val=0, max_val=SEQ)
                    pe.wait_ge(xT_evac, 4 * i + 4)

                    def gate_up(w):
                        for j in range(NF):
                            if j % 2 == 0:
                                pe.wait_ge(gu_in[j // 2], 32 * i + 32)
                            pe.wait_ge(glu_read, 8 * i + j + 1)
                            for h in range(2):
                                for k in range(KD):
                                    ins = pe.matmul(bank(j % 2)[:, 256 * h:256 * h + w],
                                                    gu_w[j // 2][:, h, k, P * (j % 2):P * (j % 2) + P],
                                                    xT[:, k, 0:w], start=(k == 0), stop=(k == KD - 1))
                            ins.then_inc(gu_done, 1)

                    def down(w):
                        pe.wait_ge(act_ready, 8 * i + 2 + NF - 2)
                        for m in range(KD):
                            if m % 2 == 0:
                                pe.wait_ge(down_in[m // 2], 16 * i + 16)
                            pe.wait_ge(yT_evac, 8 * i + m + 1)
                            for k in range(NF):
                                if m == 0 and k >= NF - 2:
                                    pe.wait_ge(act_ready, 8 * i + 2 + k + 1)
                                ins = pe.matmul(bank(6 + m % 2)[:, 0:w],
                                                down_w[m // 2][:, k, P * (m % 2):P * (m % 2) + P],
                                                actT[:, k, 0:w], start=(k == 0), stop=(k == NF - 1))
                            ins.then_inc(yT_ps, 1)

                    def item(w):
                        gate_up(w)
                        pe.wait_ge(y_evac, 4 * i + 1)
                        turn_rows(i + 1)
                        down(w)

                    by_width(n, WIDTHS, item)
                    pe.load(n_next, item_n[0:1, bass.ds(i + 1, 1)])
                    pe.wait_ge(xT_evac, 4 * i + 8)
                    for q in range(4):
                        pe.wait_ge(yT_evac, 8 * i + 6 + 4 * (q % 2))
                        for m in range(4):
                            ins = pe.transpose(bank(2 + q)[:, P * m:P * m + P],
                                               yT[:, 4 * (q % 2) + m, P * (q // 2):P * (q // 2) + P], ident[:, :])
                        ins.then_inc(y_ps, 1)

        @block.scalar
        def _(act):
            step = Steps(act, act_step)
            def square_x(t):
                act.wait_ge(x_in[t], 16)
                if t >= 2:
                    act.wait_ge(squared, t - 1)
                act.activation(squares[:, t % 2, :], x_raw[:, t, :], ACT.Square, accum_out=ssq[:, t:t + 1]) \
                   .then_inc(squared, 1)

            act.dma_start(vec_rows[V_GA:V_GA + KD, :], norm_attn_g.rearrange("l (k p) -> (l k) p", p=P)) \
               .then_inc(gain_rows_in, 16)
            for t in range(4):
                square_x(t)
            for ap, row, n in ((norm_ffn_g, V_GF, 8), (diff_norm_g, V_GD, 4),
                               (mlstm_norm_g, V_GM, 4), (mlstm_conv_b, V_CB, 4), (mlstm_o_b, V_OB, 4)):
                act.dma_start(vec_rows[row:row + n, :], ap.rearrange("l (k p) -> (l k) p", p=P)).then_inc(small_in, 16)
            act.dma_start(vec_rows[V_CW:V_CW + 16, :], mlstm_conv_w.rearrange("l c (k p) -> (l c k) p", p=P)) \
               .then_inc(small_in, 16)
            act.wait_ge(gate_bias_clear, 1)
            act.dma_start(gate_bias[0:4, :], mlstm_gate_b[:, 0:4].rearrange("l (g o) -> (l g) o", o=1)) \
               .then_inc(small_in, 16)
            act.dma_start(gate_bias[32:36, :], mlstm_gate_b[:, 4:8].rearrange("l (g o) -> (l g) o", o=1)) \
               .then_inc(small_in, 16)
            act.dma_start(table[:, :], rel_bias_table).then_inc(table_in, 16)
            act.dma_start(one_hot, buckets).then_inc(table_in, 16)
            for t in range(4, NT):
                square_x(t)

            def take_strip():
                for half in range(2):
                    act.wait_ge(strip_ps, half + 1)
                    act.activation(strip_row[:, HALF * half:HALF * half + HALF], bank(6 + half)[0:DAH, :],
                                   ACT.Copy).then_inc(strip_row_ready, 1)

            for o, (kind, a, b) in enumerate(outs):
                act.wait_ge(proj_done, o + 1)
                if o == 0:
                    act.wait_ge(squared, NT)
                cols = slice(HALF * a, HALF * a + HALF)
                if kind == QKM:
                    ins = act.activation(ml_raw[:, b, cols], bank(o % 4), ACT.Copy)
                elif kind == GATE:
                    ins = act.activation(gate_rows[0:36, cols], bank(o % 4)[0:36, :], ACT.Identity,
                                         bias=gate_bias[0:36, :])
                elif kind == Q:
                    if (a, b) == (0, 0):
                        act.wait_ge(strip_out, 16)
                    ins = act.activation(da_q[:, b, cols], bank(o % 4), ACT.Copy, scale=DQ ** -0.5)
                elif kind == K:
                    ins = act.activation(da_k[:, b, cols], bank(o % 4), ACT.Copy)
                elif kind == V:
                    if b == 0:
                        act.wait_ge(cols_ready, 2)
                        act.wait_ge(wide_ready, 8)
                    ins = act.activation(da_v[:, b, :], bank(o % 4), ACT.Copy)
                elif kind == MV:
                    ins = act.activation(ml_v[:, b, :, 0:DV], kn(bank(o % 4), MLH), ACT.Copy)
                else:
                    act.wait_ge(vec_ready, 2)
                    ins = act.activation(o_gate[:, b, cols], bank(o % 4), ACT.Sigmoid,
                                         bias=vec[:, V_OB + b:V_OB + b + 1])
                ins.then_inc(proj_evac, 1)
                if o == 3:
                    take_strip()
                if o + 1 == after_group[GATE]:
                    act.wait_ge(proj_evac, o + 1)
                    step.do(act.activation(row_a, gate_rows[32:36, :], ACT.Abs))
                    step.do(act.activation(row_a, row_a, ACT.Exp, scale=-1.0))
                    act.activation(row_a, row_a, ACT.Ln, bias=ones[0:MLH, 0:1]).then_inc(log_f_part, 1)
                if o + 1 == after_group[Q]:
                    for m in range(4):
                        act.wait_ge(conv_done, m + 1)
                        act.activation(ml_sig[:, m, :], ml_qk[:, m, :], ACT.Sigmoid).then_inc(sig_done, 1)
                if o + 1 == after_group[K]:
                    act.wait_ge(em_in, 1)
                    act.activation(row_b, row_b, ACT.Exp, scale=-1.0).then_inc(em_ready, 1)
                    act.wait_ge(qk_done, 4)
                    for n in range(8):
                        act.wait_ge(wide_ps, n + 1)
                        act.activation(m_wide[:, n // 2, HALF * (n % 2):HALF * (n % 2) + HALF], bank(6 + n % 2),
                                       ACT.Copy).then_inc(wide_ready, 1)

            for n in range(8):
                act.wait_ge(strip_flipped, n + 1)
                act.activation(strip[:, n // 2, HALF * (n % 2):HALF * (n % 2) + HALF], bank(6 + n % 2),
                               ACT.Copy).then_inc(strip_ready, 1)
            act.wait_ge(lam_ready, 1)
            act.activation(lam[:, 2:4], lam[:, 0:2], ACT.Exp).then_inc(lam_exp, 1)

            def ml_square(t):
                act.wait_ge(ml_divided, t + 1)
                for h in range(MLH):
                    act.activation(ml_sq[:, h, :], ml_hr[:, h, :], ACT.Square,
                                   accum_out=small[:, h:h + 1]).then_inc(ml_squared, 1)

            for u, (t, h, js) in enumerate(ml_units):
                if u >= 3:
                    act.wait_ge(ml_w_ready, u - 2)
                for n, j in enumerate(js):
                    if j == t:
                        act.wait_ge(ml_e_ready, MLH * t + h + 1)
                        src, bias = ml_e[:, (MLH * t + h) % 2, :], 0.0
                        ins = act.activation(ml_decay[u % 3][:, P * n:P * n + P], src, ACT.Exp, scale=-1.0)
                    else:
                        ins = act.activation(ml_decay[u % 3][:, P * n:P * n + P], m_wide[:, h, P * t:P * t + P],
                                             ACT.Exp, bias=a_col[:, j, h:h + 1], scale=-1.0)
                ins.then_inc(ml_d_ready, 1)

                for n in range(NT - 1):
                    if u == ml_tile_end[n] + 2:
                        ml_square(n)

            def da_exps(u):
                t, h = da_units[u]
                w = P * (t + 1)
                for m in range(2):
                    act.wait_ge(da_max, 2 * u + m + 1)
                    p = prob[u % 3][m][:, 0:w]
                    act.activation(p, p, ACT.Exp, bias=small[:, 8 + 4 * (u % 2) + m:9 + 4 * (u % 2) + m],
                                   accum_out=small[:, 10 + 4 * (u % 2) + m:11 + 4 * (u % 2) + m]).then_inc(da_exp, 1)

            g = 0
            for u in range(len(da_units) + 2):
                for js in (da_groups[u - 2] if u >= 2 else ()):
                    act.wait_ge(da_aT_ps, g + 1)
                    w = P * len(js)
                    act.activation(probT[:, g % 2, 0:w], bank(4 + g % 2)[:, 0:w], ACT.Copy).then_inc(da_aT_ready, 1)
                    g += 1
                if u < len(da_units):
                    da_exps(u)
                if u == 0:
                    ml_square(NT - 1)
                if u % DAH == 1 and u > DAH:
                    t = u // DAH - 1
                    act.wait_ge(da_o_done, DAH * t + DAH)
                    if t:
                        act.wait_ge(da_turned, t)
                    act.activation(da_o, kn(bank(6), DAH), ACT.Copy).then_inc(da_o_read, 1)
                    act.wait_ge(da_o_read, t + 1)
                    for h in range(DAH):
                        act.activation(da_sq[:, h, :], da_o[:, h, :], ACT.Square,
                                       accum_out=small[:, h:h + 1]).then_inc(da_squared, 1)
            for t in range(NT):
                act.wait_ge(top_ready, t + 1)
                act.activation(gate[:, t, :], top8[:, 0:TOP_K], ACT.Exp, bias=small[:, 16:17],
                               accum_out=small[:, 17:18]).then_inc(gate_exp, 1)
            act.wait_ge(g_turned, 1)
            act.wait_ge(bias_clear, 1)
            for b in range(2):
                act.activation(g_allT[0:N_EXP, 4 * b:4 * b + 4, :], kn(bank(4 + b)[0:N_EXP, :], 4),
                               ACT.Copy).then_inc(g_allT_ready, 1)

            act.sem_inc(yT_evac, 2)
            act.sem_inc(y_evac, 1)
            act.sem_inc(lin_read, 2)
            act.sem_inc(y_sent, 1)
            act.wait_ge(items_ready, 1)
            last = act.value_load(n_items[0:1, 0:1], min_val=N_EXP, max_val=ITEMS)
            with act.Fori(0, ITEMS) as i:
                with act.If(i < last):
                    act.wait_ge(cur_b_ready, i + 1)
                    for j in range(NF):
                        act.wait_ge(gu_done, 8 * i + j + 1)
                        act.wait_ge(act_ready, 8 * i + j + 1)
                        act.activation(lin_b[:, j % 2, :], bank(j % 2)[:, 256:512], ACT.Identity,
                                       bias=cur_b[:, NF + j:NF + j + 1]).then_inc(lin_read, 1)
                        act.wait_ge(glu_read, 8 * i + j + 3)
                        act.activation(glu_s[:, j % 2, :], glu_t[:, j % 2, :], ACT.Sigmoid,
                                       scale=ALPHA).then_inc(sig_ready, 1)
                    act.wait_ge(y_ps, 4 * i + 1)
                    for m in range(KD):
                        act.wait_ge(yT_ps, 8 * i + m + 2)
                        act.activation(yT[:, m, :], bank(6 + m % 2)[:, 0:ITEM], ACT.Copy).then_inc(yT_evac, 1)
                    act.wait_ge(y_sent, i + 1)
                    for q in range(4):
                        act.wait_ge(y_ps, 4 * i + q + 2)
                        act.activation(y_rows[:, q // 2, HALF * (q % 2):HALF * (q % 2) + HALF], bank(2 + q),
                                       ACT.Copy).then_inc(y_evac, 1)
            for t in range(NT + 1):
                if t < NT:
                    act.wait_ge(y_sum, t + 1)
                    if t >= 2:
                        act.wait_ge(sum_squared, t - 1)
                    act.activation(sum_squares[:, t % 2, :], x1[:, t, :], ACT.Square,
                                   accum_out=ssq[:, t:t + 1]).then_inc(sum_squared, 1)
                if t:
                    act.wait_ge(out_ready, t)
                    act.dma_start(out_rows[t - 1], out_sb[:, (t - 1) % 3, :]).then_inc(out_sent[(t - 1) % 3], 16)

        @block.vector
        def _(dve):
            step = Steps(dve, dve_step)

            def mean_square(t):
                dve.wait_ge(squared, t + 1)
                dve.tensor_scalar(ssq[:, t:t + 1], ssq[:, t:t + 1], 1.0 / D, EPS, ALU.mult, ALU.add).then_inc(mean_sq, 1)

            def scale_x(t):
                dve.wait_ge(rstd_ready, t + 1)
                dve.tensor_scalar(x_raw[:, t, :], x_raw[:, t, :], rstd[:, t:t + 1], None, ALU.mult).then_inc(x_scaled, 1)

            mean_square(0)
            mean_square(1)
            scale_x(0)
            for t in range(NT):
                if t + 1 < NT:
                    scale_x(t + 1)
                if t == 0:
                    dve.wait_ge(vec_ps, 1)
                    dve.tensor_copy(vec[:, 0:KD], bank(0)[:, 0:KD]).then_inc(vec_ready, 1)
                    dve.wait_ge(vec_ready, 1)
                dve.wait_ge(x_turned, t + 1)
                for kb in range(2):
                    ins = dve.tensor_tensor(hT[:, 4 * kb:4 * kb + 4, P * t:P * t + P],
                                            kn(bank(4 + 2 * (t % 2) + kb), 4),
                                            wide(vec[:, V_GA + 4 * kb:V_GA + 4 * kb + 4], P), ALU.mult)
                ins.then_inc(hT_ready, 1)
                if t + 2 < NT:
                    mean_square(t + 2)

            dve.wait_ge(vec_ps, 2)
            dve.tensor_copy(vec[:, KD:V_ROWS], bank(5)[:, KD:V_ROWS]).then_inc(vec_ready, 1)
            dve.wait_ge(vec_ready, 2)
            dve.wait_ge(lam_in_sem, 64)
            for n in range(2):
                step.do(dve.tensor_tensor_reduce(lam_in[:, 2 * n, :], lam_in[:, 2 * n, :], lam_in[:, 2 * n + 1, :], 1.0, 0.0,
                                                 ALU.mult, ALU.add, lam[:, n:n + 1]))
            dve.tensor_scalar(gd_scaled[:, :], vec[:, V_GD:V_GD + 4], 1.0 - LAM_INIT, None,
                              ALU.mult).then_inc(lam_ready, 1)

            dve.wait_ge(log_f_part, 1)
            step.do(dve.tensor_scalar(row_b, gate_rows[32:36, :], 0.0, None, ALU.min))
            step.do(dve.tensor_tensor(row_b, row_b, row_a, ALU.subtract))

            def running(src, dst, op):
                s = 1
                while s < SEQ:
                    dve.tensor_tensor(dst[:, s:], src[:, s:], src[:, :SEQ - s], op)
                    step.do(dve.tensor_copy(dst[:, 0:s], src[:, 0:s]))
                    src, dst = dst, src
                    s *= 2

            running(row_b, row_a, ALU.add)
            step.do(dve.tensor_tensor(row_c, row_g, row_b, ALU.subtract))
            step.do(dve.tensor_scalar(row_a, row_c, 0.0, None, ALU.max))
            running(row_a, row_g, ALU.max)
            dve.tensor_tensor(row_b, row_b, row_a, ALU.add).then_inc(em_in, 1)
            dve.wait_ge(proj_evac, after_group[GATE])
            for m in range(4):
                def tap(n):
                    return vec[:, V_CW + 4 * n + m:V_CW + 4 * n + m + 1]
                step.do(dve.tensor_scalar(ml_qk[:, m, :], ml_raw[:, m, :], tap(3), vec[:, V_CB + m:V_CB + m + 1],
                                          ALU.mult, ALU.add))
                for s in range(1, 4):
                    ins = dve.scalar_tensor_tensor(out=ml_qk[:, m, s:], in0=ml_raw[:, m, :SEQ - s], scalar=tap(3 - s),
                                                   in1=ml_qk[:, m, s:], op0=ALU.mult, op1=ALU.add)
                    if s < 3:
                        step.do(ins)
                    else:
                        ins.then_inc(conv_done, 1)
            for m in range(4):
                dve.wait_ge(sig_done, m + 1)
                dve.scalar_tensor_tensor(out=ml_qk[:, m, :], in0=ml_qk[:, m, :], scalar=1.0 if m < 2 else DQ ** -0.5,
                                         in1=ml_sig[:, m, :], op0=ALU.mult, op1=ALU.mult).then_inc(qk_done, 1)
            dve.wait_ge(cols_ps, 1)
            dve.tensor_copy(a_col[:, :, :], kn(bank(4)[:, 0:32])).then_inc(cols_ready, 1)
            dve.tensor_copy(em_col[:, :, :], kn(bank(4)[:, 32:64])).then_inc(cols_ready, 1)
            dve.wait_ge(proj_evac, N_OUTS)
            dve.memset(ml_v[:, :, :, DV:DV + 1], 1.0).then_inc(v_ones, 1)
            step.do(dve.tensor_tensor(o_gate, o_gate, wide(vec[:, V_GM:V_GM + 4], SEQ), ALU.mult))
            dve.wait_ge(lam_exp, 1)
            step.do(dve.tensor_tensor(lam[:, 0:1], lam[:, 3:4], lam[:, 2:3], ALU.subtract))
            step.do(dve.tensor_scalar(lam[:, 1:2], lam[:, 0:1], -LAM_INIT, None, ALU.add))

            def head_mean_square(squared_heads, tiles):
                dve.wait_ge(squared_heads, MLH * tiles)
                dve.tensor_scalar(small[:, 0:4], small[:, 0:4], 1.0 / DV, EPS, ALU.mult, ALU.add).then_inc(mean_sq, 1)

            def ml_take(t):
                dve.wait_ge(ml_h_done, ml_tile_end[t])
                for b in range(2):
                    ins = dve.tensor_copy(ml_h[:, 2 * b:2 * b + 2, :],
                                          bank(2 + 2 * (t % 2) + b)[:, 0:2 * (DV + 1)].rearrange("p (h d) -> p h d", h=2))
                ins.then_inc(ml_h_read, 1)
                dve.wait_ge(ml_h_read, t + 1)
                step.do(dve.scalar_tensor_tensor(out=small[:, 20:24], in0=ml_h[:, :, DV], scalar=-1.0,
                                                 in1=ml_h[:, :, DV], op0=ALU.mult, op1=ALU.max))
                step.do(dve.tensor_tensor(small[:, 20:24], small[:, 20:24], em_col[:, t, :], ALU.max))
                step.do(dve.reciprocal(small[:, 24:28], small[:, 20:24]))

            def ml_divide(t):
                if t:
                    dve.wait_ge(ml_turned, t)
                dve.tensor_tensor(ml_hr, ml_h[:, :, 0:DV], wide(small[:, 24:28], DV), ALU.mult).then_inc(ml_divided, 1)

            def ml_mean(t):
                head_mean_square(ml_squared, t + 1)

            def ml_norm(t):
                dve.wait_ge(rstd_ready, NT + t + 1)
                dve.tensor_tensor(ml_hr, ml_hr, wide(small[:, 4:8], DV), ALU.mult).then_inc(ml_norm_ready, 1)

            def ml_mix(t):
                dve.wait_ge(ml_turned, t + 1)
                dve.tensor_tensor(mixT[:, 4:8, P * t:P * t + P], kn(bank(7), 4), o_gate[:, :, P * t:P * t + P],
                                  ALU.mult).then_inc(ml_mixed, 1)

            def ml_diag(u):
                if u not in ml_diagonal:
                    return
                n = ml_diagonal.index(u)
                t, h, _ = ml_units[u]
                if n >= 2:
                    dve.wait_ge(ml_d_ready, ml_diagonal[n - 2] + 1)
                dve.scalar_tensor_tensor(out=ml_e[:, n % 2, :], in0=m_wide[:, h, P * t:P * t + P],
                                         scalar=a_col[:, t, h:h + 1], in1=above, op0=ALU.subtract,
                                         op1=ALU.max).then_inc(ml_e_ready, 1)

            dve.wait_ge(consts, 7)
            ml_diag(0)
            for u, (t, h, js) in enumerate(ml_units):
                ml_diag(u + 1)
                dve.wait_ge(ml_s_done, u + 1)
                dve.wait_ge(ml_d_ready, u + 1)
                if u >= 3:
                    dve.wait_ge(ml_h_done, u - 2)
                w = P * len(js)
                dve.tensor_tensor(ml_w[u % 3][:, 0:w], bank(ml_bank[u % 3])[:, 0:w], ml_decay[u % 3][:, 0:w],
                                  ALU.mult).then_inc(ml_w_ready, 1)
                for n in range(NT - 1):
                    for k, part in enumerate((ml_take, ml_divide, ml_mean, ml_norm, None, ml_mix)):
                        if part and u == ml_tile_end[n] + k:
                            part(n)
            ml_take(NT - 1)

            def da_softmax_in(u):
                t, h = da_units[u]
                w = P * (t + 1)
                s = 8 + 4 * (u % 2)
                if u == 0:
                    dve.wait_ge(strip_ready, 8)
                if u >= 3:
                    dve.wait_ge(da_aT_ps, sum(len(x) for x in da_groups[:u - 2]))
                for m in range(2):
                    dve.wait_ge(da_logits, 2 * u + m + 1)
                    step.do(dve.tensor_tensor_reduce(prob[u % 3][m][:, 0:w], banks2(2 * m)[:, 0:w],
                                                     strip[:, h, SEQ - w:SEQ], 1.0, 3 * MASKED, ALU.add, ALU.max,
                                                     small[:, 28 + m:29 + m]))
                    dve.tensor_scalar(small[:, s + m:s + m + 1], small[:, 28 + m:29 + m], -1.0, None,
                                      ALU.mult).then_inc(da_max, 1)

            def da_combine(u):
                t, h = da_units[u]
                w = P * (t + 1)
                s = 8 + 4 * (u % 2)
                dve.wait_ge(da_exp, 2 * u + 2)
                if u:
                    dve.wait_ge(da_a_ready, u)
                step.do(dve.reciprocal(small[:, 20:22], small[:, s + 2:s + 4]))
                step.do(dve.tensor_tensor(small[:, 22:23], small[:, 21:22], lam[:, 1:2], ALU.mult))
                p0, p1 = prob[u % 3][0][:, 0:w], prob[u % 3][1][:, 0:w]
                step.do(dve.tensor_scalar(p1, p1, small[:, 22:23], None, ALU.mult))
                dve.scalar_tensor_tensor(out=p0, in0=p0, scalar=small[:, 20:21], in1=p1, op0=ALU.mult,
                                         op1=ALU.add).then_inc(da_a_ready, 1)

            def da_mean(t):
                head_mean_square(da_squared, t + 1)

            def da_norm(t):
                dve.wait_ge(rstd_ready, 2 * NT + t + 1)
                dve.tensor_tensor(da_o, da_o, wide(small[:, 4:8], DV), ALU.mult).then_inc(da_norm_ready, 1)

            def da_mix(t):
                dve.wait_ge(da_turned, t + 1)
                dve.tensor_tensor(mixT[:, 0:4, P * t:P * t + P], kn(bank(7), 4), wide(gd_scaled[:, :], P),
                                  ALU.mult).then_inc(da_mixed, 1)

            da_softmax_in(0)
            ml_divide(NT - 1)
            da_combine(0)
            da_softmax_in(1)
            ml_mean(NT - 1)
            da_combine(1)
            ml_norm(NT - 1)
            ml_mix(NT - 1)
            da_softmax_in(2)
            for u in range(3, len(da_units) + 1):
                da_combine(u - 1)
                if u < len(da_units):
                    da_softmax_in(u)
                if u % DAH == 2 and u > DAH:
                    da_mean(u // DAH - 1)
                if u % DAH == 3 and u > DAH:
                    da_norm(u // DAH - 1)
                if u % DAH == 1 and u > 2 * DAH:
                    da_mix(u // DAH - 2)
            da_mix(NT - 2)
            da_mean(NT - 1)
            da_norm(NT - 1)
            da_mix(NT - 1)

            def residual(t):
                dve.wait_ge(out_proj_done, t + 1)
                dve.wait_ge(x_again_in[t % 2], 16 * (t // 2 + 1))
                dve.tensor_tensor(x1[:, t, :], banks2(2 * (t % 2)), x_again[:, t % 2, :], ALU.add).then_inc(x1_ready, 1)
                dve.wait_ge(x1_ready, t + 1)
                if t >= 2:
                    dve.wait_ge(h2_out[t % 2], 16 * (t // 2))
                step.do(dve.tensor_tensor_reduce(h2[:, t % 2, :], x1[:, t, :], x1[:, t, :], 1.0, 0.0, ALU.mult, ALU.add,
                                                 ssq[:, t:t + 1]))
                dve.tensor_scalar(ssq[:, t:t + 1], ssq[:, t:t + 1], 1.0 / D, EPS, ALU.mult, ALU.add).then_inc(mean_sq, 1)
                dve.wait_ge(rstd_ready, 3 * NT + t + 1)
                dve.tensor_scalar(h2[:, t % 2, :], x1[:, t, :], rstd[:, t:t + 1], None, ALU.mult).then_inc(h2_ready, 1)
                for kb in range(2):
                    dve.wait_ge(h2_turned, 2 * t + kb + 1)
                    dve.tensor_tensor(h2T[t % 2][:, 4 * kb:4 * kb + 4, :], kn(bank(4 + kb), 4),
                                      wide(vec[:, V_GF + 4 * kb:V_GF + 4 * kb + 4], P), ALU.mult).then_inc(h2T_ready, 1)

            def choose(t):
                dve.wait_ge(logits_done, t + 1)
                if t == 0:
                    dve.wait_ge(row_ids, 2)
                    dve.wait_ge(router_in, 32)
                step.do(dve.tensor_tensor(lg[:, :], bank(6)[:, 0:N_EXP], rb_wide[:, :], ALU.add))
                step.do(dve.max(top8[:, :], lg[:, :]))
                step.do(dve.max_index(idx8[:, :], top8[:, :], lg[:, :]))
                step.do(dve.tensor_copy(idxf[:, t, :], idx8[:, 0:TOP_K]))
                dve.tensor_scalar(small[:, 16:17], top8[:, 0:1], -1.0, None, ALU.mult).then_inc(top_ready, 1)
                for c in range(TOP_K):
                    ins = dve.tensor_scalar(chosen[:, t, c, :], lanes[:, :], idxf[:, t, c:c + 1], None, ALU.is_equal)
                step.do(ins)
                step.do(dve.tensor_reduce(mask[:, t, :], chosen[:, t, :, :].rearrange("p c e -> p e c"), AX, ALU.add))
                dve.wait_ge(gate_exp, t + 1)
                step.do(dve.reciprocal(small[:, 18:19], small[:, 17:18]))
                step.do(dve.tensor_scalar(gate[:, t, :], gate[:, t, :], small[:, 18:19], None, ALU.mult))
                step.do(dve.tensor_scalar(g_all[:, t, :], chosen[:, t, 0, :], gate[:, t, 0:1], None, ALU.mult))
                for c in range(1, TOP_K):
                    ins = dve.scalar_tensor_tensor(out=g_all[:, t, :], in0=chosen[:, t, c, :], scalar=gate[:, t, c:c + 1],
                                                   in1=g_all[:, t, :], op0=ALU.mult, op1=ALU.add)
                    if c < TOP_K - 1:
                        step.do(ins)
                ins.then_inc(chosen_ready, 1)

            def slots(t):
                dve.wait_ge(pos_ps, t + 1)
                if t == NT - 1:
                    step.do(dve.tensor_copy(counts[:, :], bank(7)[:, N_EXP:2 * N_EXP]))
                dve.tensor_tensor(chosen[:, t, :, :], chosen[:, t, :, :], again(bank(7)[:, 0:N_EXP], TOP_K),
                                  ALU.mult).then_inc(place_read, 1)
                dve.wait_ge(place_read, t + 1)
                step.do(dve.tensor_reduce(slot[:, t, :], chosen[:, t, :, :], AX, ALU.add))
                step.do(dve.tensor_copy(slot_i[:, t, :], slot[:, t, :]))
                dve.tensor_scalar(slot_lo[:, t, :], slot_i[:, t, :], P - 1, 8, ALU.bitwise_and, ALU.logical_shift_left)
                step.do(dve.tensor_scalar(slot_hi[:, t, :], slot_i[:, t, :], 7, None, ALU.logical_shift_right))
                step.do(dve.tensor_tensor(slot[:, t, :], slot_hi[:, t, :], slot_lo[:, t, :], ALU.add))
                dve.scalar_tensor_tensor(out=where[:, t, :], in0=idxf[:, t, :], scalar=float(LISTS), in1=slot[:, t, :],
                                         op0=ALU.mult, op1=ALU.add).then_inc(where_ready, 1)

            def add_down_bias(t):
                dve.wait_ge(down_bias_done, t + 1)
                dve.tensor_tensor(x1[:, t, :], x1[:, t, :], banks2(2 * (t % 2)), ALU.add).then_inc(x1_full, 1)

            residual(0)
            for t in range(NT):
                if t + 1 < NT:
                    residual(t + 1)
                choose(t)
                if t:
                    slots(t - 1)
                if t == NT - 1:
                    dve.memset(pairA[:, 6144:8192], 0.0).then_inc(bias_clear, 1)
                if t == NT - 2:
                    dve.wait_ge(b_gu_turned, 1)
                    dve.tensor_copy(b_gu[:, :, :].rearrange("p e f -> p f e"),
                                    bank(0).rearrange("p (f e) -> p f e", e=N_EXP)).then_inc(b_gu_ready, 1)
            slots(NT - 1)

            R, N = ROUNDS, ROUNDS * N_EXP
            dve.wait_ge(item_iotas, 2)
            for r in range(R):
                dve.tensor_scalar(flag[:, N_EXP * r:N_EXP * (r + 1)], counts[0:1, :], float(ITEM * (r + 1)), None,
                                  ALU.is_gt)
                ins = dve.tensor_scalar(packed[:, N_EXP * r:N_EXP * (r + 1)], counts[0:1, :],
                                        float(-ITEM * (r + 1)), 256.0, ALU.add, ALU.mult)
            step.do(ins)
            dve.tensor_copy(pos, flag)
            step.do(dve.tensor_tensor(packed, packed, val_c, ALU.add))
            step.do(dve.tensor_tensor(packed, packed, flag, ALU.mult))
            src, dst, s = pos, pos2, 1
            while s < N:
                dve.tensor_tensor(dst[:, s:], src[:, s:], src[:, :N - s], ALU.add)
                step.do(dve.tensor_copy(dst[:, 0:s], src[:, 0:s]))
                src, dst, s = dst, src, 2 * s
            step.do(dve.tensor_tensor(eq, again(src, MAX_EXTRA), order, ALU.is_equal))
            step.do(dve.tensor_tensor(eq, eq, again(packed, MAX_EXTRA), ALU.mult))
            step.do(dve.tensor_reduce(got, eq, AX, ALU.add))
            step.do(dve.tensor_copy(got_i[:, :], got))
            extra = slice(N_EXP, N_EXP + MAX_EXTRA)
            dve.tensor_copy(item_e[0:1, 0:N_EXP], lanes[0:1, :])
            dve.tensor_scalar(item_col[0:1, 0:N_EXP], lanes[0:1, :], float(LISTS), None, ALU.mult)
            dve.tensor_copy(item_n[0:1, 0:N_EXP], counts[0:1, :])
            for tab in (item_e, item_col, item_n):
                dve.memset(tab[0:1, ITEMS:ITEMS + 1], 0)
            dve.tensor_scalar(item_n[0:1, extra], got_i[:, :], 8, None, ALU.logical_shift_right)
            step.do(dve.tensor_scalar(item_col[0:1, extra], got_i[:, :], 255, None, ALU.bitwise_and))
            dve.tensor_scalar(item_e[0:1, extra], item_col[0:1, extra], 3, None, ALU.logical_shift_right)
            dve.tensor_scalar(n_items[:, :], src[:, N - 1:N], float(N_EXP), None, ALU.add).then_inc(items_ready, 1)
            dve.wait_ge(list_in, 16)
            dve.tensor_scalar(x_idx[:, :], y_idx[:, :], 2, None, ALU.logical_shift_right).then_inc(x_idx_ready, 1)
            dve.wait_ge(x_idx_ready, 1)
            dve.tensor_copy(cur_x[:, :], x_idx[:, 0:2]).then_inc(cur_x_ready, 1)

            for t in range(NT):
                add_down_bias(t)
            dve.wait_ge(items_ready, 1)
            last = dve.value_load(n_items[0:1, 0:1], min_val=N_EXP, max_val=ITEMS)

            def take_xT(i):
                for q in range(4):
                    dve.wait_ge(xT_ps, 4 * i + q + 1)
                    dve.tensor_tensor(xT[:, 2 * q:2 * q + 2, :], kn(bank(2 + q), 2),
                                      wide(vec[:, V_GF + 2 * q:V_GF + 2 * q + 2], ITEM), ALU.mult).then_inc(xT_evac, 1)

            take_xT(0)
            dve.sem_inc(glu_read, 2)
            dve.sem_inc(act_ready, 2)
            per_item = NF * 2
            start = step.n
            with dve.Fori(0, ITEMS) as i:
                with dve.If(i < last):
                    step.base, step.n = start + per_item * i, 0
                    e = dve.value_load(item_e[0:1, bass.ds(i, 1)], min_val=0, max_val=N_EXP - 1)
                    col = dve.value_load(item_col[0:1, bass.ds(i, 1)], min_val=0, max_val=N_EXP * LISTS - 2)
                    nxt = dve.value_load(item_col[0:1, bass.ds(i + 1, 1)], min_val=0, max_val=N_EXP * LISTS - 2)
                    dve.wait_ge(lin_read, 8 * i + 2)
                    dve.tensor_copy(cur_b[:, :], b_gu[:, bass.ds(e, 1), :]).then_inc(cur_b_ready, 1)
                    dve.wait_ge(xg_in, 32 * i + 32)
                    dve.tensor_copy(cur_x[:, :], x_idx[:, bass.ds(nxt, 2)]).then_inc(cur_x_ready, 1)
                    dve.wait_ge(cur_b_ready, i + 1)
                    dve.wait_ge(yT_ps, 8 * i + 1)
                    for j in range(NF):
                        dve.wait_ge(lin_read, 8 * i + j + 3)
                        dve.tensor_scalar(glu_t[:, j % 2, :], bank(j % 2)[:, 0:256], cur_b[:, j:j + 1], LIMIT,
                                          ALU.add, ALU.min).then_inc(glu_read, 1)
                        step.do(dve.tensor_scalar(lin_c[:, j % 2, :], lin_b[:, j % 2, :], LIMIT, -LIMIT,
                                                  ALU.min, ALU.max))
                        dve.wait_ge(sig_ready, 8 * i + j + 1)
                        step.do(dve.tensor_tensor(glu_s[:, j % 2, :], glu_t[:, j % 2, :], glu_s[:, j % 2, :], ALU.mult))
                        dve.scalar_tensor_tensor(out=actT[:, j, :], in0=lin_c[:, j % 2, :], scalar=1.0,
                                                 in1=glu_s[:, j % 2, :], op0=ALU.add, op1=ALU.mult).then_inc(act_ready, 1)
                    take_xT(i + 1)
                    dve.wait_ge(y_sent, i + 1)
                    dve.tensor_copy(cur_y[:, :], y_idx[:, bass.ds(col, 2)]).then_inc(cur_y_ready, 1)
                    assert step.n == per_item

            dve.wait_ge(y_sent, last + 1)
            dve.wait_ge(gain_in, 16)
            tail = Steps(dve, tail_step)

            def tail_mean(t):
                dve.wait_ge(sum_squared, t + 1)
                dve.tensor_scalar(ssq[:, t:t + 1], ssq[:, t:t + 1], 1.0 / D, EPS, ALU.mult, ALU.add).then_inc(mean_sq, 1)

            def tail_norm(t):
                dve.wait_ge(rstd_ready, 4 * NT + t + 1)
                if t >= 3:
                    dve.wait_ge(out_sent[t % 3], 16 * (t // 3))
                dve.scalar_tensor_tensor(out=out_sb[:, t % 3, :], in0=x1[:, t, :], scalar=rstd[:, t:t + 1],
                                         in1=gain_wide, op0=ALU.mult, op1=ALU.mult).then_inc(out_ready, 1)

            for t in range(NT):
                dve.wait_ge(y_back[t % 4], 16 * (t // 4 + 1))
                for c in range(TOP_K):
                    ins = dve.scalar_tensor_tensor(out=x1[:, t, :], in0=y_in[t % 4][:, c, :], scalar=gate[:, t, c:c + 1],
                                                   in1=x1[:, t, :], op0=ALU.mult, op1=ALU.add)
                    if c < TOP_K - 1:
                        tail.do(ins)
                    if c == 1 and t:
                        tail_mean(t - 1)
                ins.then_inc(y_sum, 1)
                if t:
                    tail_norm(t - 1)
            tail_mean(NT - 1)
            tail_norm(NT - 1)


_INS = ['x', 'norm_attn_g', 'w_in', 'rel_bias_table', 'lambda_q1', 'lambda_k1', 'lambda_q2', 'lambda_k2',
        'diff_norm_g', 'mlstm_conv_w', 'mlstm_conv_b', 'mlstm_gate_b', 'mlstm_o_b', 'mlstm_norm_g', 'w_out',
        'norm_ffn_g', 'router_w', 'router_b', 'expert_w_gu', 'expert_b_gu', 'expert_w_down', 'expert_b_down',
        'final_norm_g']


def kernel(**inputs):
    import concourse.bacc as bacc
    from concourse.bass_utils import run_bass_kernel_spmd as run

    nc = bacc.Bacc("TRN2", target_bir_lowering=False, num_devices=1)
    arrays, args = {}, []
    for name, a in [(n, inputs[n]) for n in _INS] + [("buckets", bucket_rows())]:
        a = np.ascontiguousarray(a)
        arrays[f"in_{name}_dram"] = a
        args.append(nc.dram_tensor(f"in_{name}_dram", a.shape, mybir.dt.from_np(a.dtype), kind="ExternalInput").ap())
    args.append(nc.dram_tensor("out_0_dram", (1, SEQ, D), F32, kind="ExternalOutput").ap())
    build(nc, *args)
    r = run(nc, [arrays], core_ids=[0])
    return r.results[0]["out_0_dram"]
```
